# Optimizing a Trainium2 kernel written in Bass

```python
import jax, jax.numpy as jnp
from jax import lax
import numpy as np

D_MODEL = 1024
BATCH = 1
SEQ = 256
DEPTH = 2

HEAD_DIM = 64
ROPE_THETA = 10000.0
Q_BLOCK = 128
LN_EPS = 1e-5
RMS_EPS = 1e-6

NSA_HEADS = 8
NSA_KV_HEADS = 2
NSA_CMP_LEN = 32
NSA_CMP_STRIDE = 16
NSA_CMP_HIDDEN = 128
NSA_SEL_BLOCK = 64
NSA_SEL_TOPN = 8
NSA_WINDOW = 512

MLA_HEADS = 8
MLA_Q_RANK = 256
MLA_KV_RANK = 128
MLA_NOPE_DIM = 64
MLA_ROPE_DIM = 32
MLA_V_DIM = 64

MOBA_HEADS = 16
MOBA_BLOCK = 256
MOBA_TOPK = 3
MOBA_Q_CHUNK = 32

N_EXPERTS = 64
N_GROUPS = 8
TOPK_GROUPS = 4
TOP_K = 8
EXPERT_FF = 256
SHARED_FF = 256
ROUTED_SCALE = 2.5
MOE_ROW_BLOCK = 128

DN_ALPHA = (2 * DEPTH) ** 0.25
DN_BETA = (8 * DEPTH) ** -0.25

NSA_Q_W = NSA_HEADS * HEAD_DIM
NSA_KV_W = 6 * NSA_KV_HEADS * HEAD_DIM
NSA_GATE_W = 3 * NSA_HEADS
SPLIT0 = (NSA_Q_W,
          NSA_Q_W + NSA_KV_W,
          NSA_Q_W + NSA_KV_W + NSA_GATE_W,
          NSA_Q_W + NSA_KV_W + NSA_GATE_W + MLA_Q_RANK,
          NSA_Q_W + NSA_KV_W + NSA_GATE_W + MLA_Q_RANK + MLA_KV_RANK)
IN_W0 = NSA_Q_W + NSA_KV_W + NSA_GATE_W + MLA_Q_RANK + MLA_KV_RANK + MLA_ROPE_DIM
MIX_W0 = NSA_HEADS * HEAD_DIM + MLA_HEADS * MLA_V_DIM

kernel_name = "hybrid_nsa_mla_moba_moe_deepnorm"

def layer_norm(x, g, b):
    xf = x.astype(jnp.float32)
    mu = jnp.mean(xf, -1, keepdims=True)
    var = jnp.mean(jnp.square(xf - mu), -1, keepdims=True)
    y = (xf - mu) * lax.rsqrt(var + LN_EPS) * g.astype(jnp.float32) + b.astype(jnp.float32)
    return y.astype(x.dtype)

def rms_norm(x, g):
    xf = x.astype(jnp.float32)
    y = xf * lax.rsqrt(jnp.mean(jnp.square(xf), -1, keepdims=True) + RMS_EPS)
    return (y * g.astype(jnp.float32)).astype(x.dtype)

def rope(x, pos):
    half = x.shape[-1] // 2
    inv_freq = ROPE_THETA ** (-jnp.arange(half, dtype=jnp.float32) / half)
    ang = pos.astype(jnp.float32)[:, None] * inv_freq[None, :]
    cos = jnp.cos(ang).astype(x.dtype)
    sin = jnp.sin(ang).astype(x.dtype)
    x1, x2 = x[..., :half], x[..., half:]
    return jnp.concatenate([x1 * cos - x2 * sin, x2 * cos + x1 * sin], axis=-1)

def masked_softmax(s, mask):
    s = jnp.where(mask, s.astype(jnp.float32), -jnp.inf)
    m = jnp.max(s, axis=-1, keepdims=True)
    e = jnp.exp(s - jnp.where(jnp.isfinite(m), m, 0.0))
    den = jnp.sum(e, axis=-1, keepdims=True)
    return e / jnp.where(den > 0, den, 1.0)

def seq_blocks(t, axis, size):
    n = t.shape[axis] // size
    t = t.reshape(t.shape[:axis] + (n, size) + t.shape[axis + 1:])
    return jnp.moveaxis(t, axis, 0)

def merge_blocks(t, axis):
    t = jnp.moveaxis(t, 0, axis)
    return t.reshape(t.shape[:axis] + (t.shape[axis] * t.shape[axis + 1],) + t.shape[axis + 2:])

def nsa_attention(q, kv, gate_logits, pe_k, pe_v, cmp_k1, cmp_k2, cmp_v1, cmp_v2):
    B, S, _ = q.shape
    H, G, dh = NSA_HEADS, NSA_KV_HEADS, HEAD_DIM
    R = H // G
    scale = dh ** -0.5
    pos = jnp.arange(S)
    qh = rope(q.reshape(B, S, H, dh).transpose(0, 2, 1, 3), pos).reshape(B, G, R, S, dh)
    kc, vc, ks, vs, kw, vw = [t.reshape(B, S, G, dh).transpose(0, 2, 1, 3)
                              for t in jnp.split(kv, 6, axis=-1)]

    n_cmp = (S - NSA_CMP_LEN) // NSA_CMP_STRIDE + 1
    cmp_tok = np.arange(n_cmp)[:, None] * NSA_CMP_STRIDE + np.arange(NSA_CMP_LEN)[None, :]
    cmp_end = jnp.asarray(cmp_tok[:, -1])

    def compress(t, pe, w1, w2):
        blocks = (t[:, :, cmp_tok] + pe).reshape(B, G, n_cmp, NSA_CMP_LEN * dh)
        return jax.nn.gelu(blocks @ w1) @ w2

    k_cmp = rope(compress(kc, pe_k, cmp_k1, cmp_k2), cmp_end)
    v_cmp = compress(vc, pe_v, cmp_v1, cmp_v2)
    s_cmp = jnp.einsum('bgrsd,bgcd->bgrsc', qh, k_cmp) * scale
    p_cmp = masked_softmax(s_cmp, cmp_end[None, :] <= pos[:, None])
    o_cmp = jnp.einsum('bgrsc,bgcd->bgrsd', p_cmp.astype(vc.dtype), v_cmp)

    Ls = NSA_SEL_BLOCK
    n_sel = S // Ls
    cmp_to_sel = (cmp_tok[:, :, None] // Ls == np.arange(n_sel)[None, None, :]).sum(1) / NSA_CMP_LEN
    imp = jnp.einsum('bgrsc,cj->bgsj', p_cmp, jnp.asarray(cmp_to_sel, dtype=jnp.float32))
    blk = jnp.arange(n_sel)[None, :]
    cur = (pos // Ls)[:, None]
    forced = (blk == 0) | (blk == cur) | (blk == cur - 1)
    imp = jnp.where(blk <= cur, jnp.where(forced, jnp.inf, imp), -jnp.inf)
    n_top = min(NSA_SEL_TOPN, n_sel)
    sel_val, sel_idx = lax.top_k(imp, n_top)
    sel_ok = sel_val > -jnp.inf
    ks_blk = rope(ks, pos).reshape(B, G, n_sel, Ls, dh)
    vs_blk = vs.reshape(B, G, n_sel, Ls, dh)
    bi = jnp.arange(B)[:, None, None, None]
    gi = jnp.arange(G)[None, :, None, None]

    def sel_block(args):
        qb, idx, ok, qpos = args
        qn = qb.shape[3]
        kg = ks_blk[bi, gi, idx].reshape(B, G, qn, n_top * Ls, dh)
        vg = vs_blk[bi, gi, idx].reshape(B, G, qn, n_top * Ls, dh)
        s = jnp.einsum('bgrqd,bgqkd->bgrqk', qb, kg) * scale
        kpos = idx[..., None] * Ls + jnp.arange(Ls)
        mask = (ok[..., None] & (kpos <= qpos[:, None, None])).reshape(B, G, 1, qn, n_top * Ls)
        p = masked_softmax(s, mask)
        return jnp.einsum('bgrqk,bgqkd->bgrqd', p.astype(vg.dtype), vg)

    o_sel = lax.map(sel_block, (seq_blocks(qh, 3, Q_BLOCK), seq_blocks(sel_idx, 2, Q_BLOCK),
                                seq_blocks(sel_ok, 2, Q_BLOCK), pos.reshape(-1, Q_BLOCK)))
    o_sel = merge_blocks(o_sel, 3)

    nqb = S // Q_BLOCK
    nw = NSA_WINDOW // Q_BLOCK
    band_idx = np.arange(nqb)[:, None] + np.arange(nw + 1)[None, :]

    def band(t):
        tp = jnp.pad(t, ((0, 0), (0, 0), (NSA_WINDOW, 0), (0, 0))).reshape(B, G, nqb + nw, Q_BLOCK, dh)
        return tp[:, :, band_idx].reshape(B, G, nqb, (nw + 1) * Q_BLOCK, dh)

    k_band = band(rope(kw, pos))
    v_band = band(vw)
    s_w = jnp.einsum('bgrnqd,bgnkd->bgrnqk', qh.reshape(B, G, R, nqb, Q_BLOCK, dh), k_band) * scale
    qpos = pos.reshape(nqb, Q_BLOCK)
    kpos = (jnp.arange(nqb)[:, None] - nw) * Q_BLOCK + jnp.arange((nw + 1) * Q_BLOCK)[None, :]
    diff = qpos[:, :, None] - kpos[:, None, :]
    mask_w = (diff >= 0) & (diff < NSA_WINDOW) & (kpos[:, None, :] >= 0)
    p_w = masked_softmax(s_w, mask_w)
    o_win = jnp.einsum('bgrnqk,bgnkd->bgrnqd', p_w.astype(vw.dtype), v_band).reshape(B, G, R, S, dh)

    g = jax.nn.sigmoid(gate_logits.astype(jnp.float32)).astype(q.dtype)
    g = g.reshape(B, S, 3, G, R).transpose(2, 0, 3, 4, 1)[..., None]
    o = g[0] * o_cmp + g[1] * o_sel + g[2] * o_win
    return o.reshape(B, H, S, dh).transpose(0, 2, 1, 3).reshape(B, S, H * dh)

def causal_attention_blocks(q, k, v, scale):
    S = q.shape[2]
    kpos = jnp.arange(S)

    def one(args):
        qb, qp = args
        s = jnp.einsum('bhqd,bhkd->bhqk', qb, k) * scale
        p = masked_softmax(s, kpos[None, :] <= qp[:, None])
        return jnp.einsum('bhqk,bhkd->bhqd', p.astype(v.dtype), v)

    o = lax.map(one, (seq_blocks(q, 2, Q_BLOCK), kpos.reshape(-1, Q_BLOCK)))
    return merge_blocks(o, 2)

def mla_attention(c_q, c_kv, k_rope, q_norm_g, w_uq, kv_norm_g, w_ukv):
    B, S, _ = c_q.shape
    H = MLA_HEADS
    pos = jnp.arange(S)
    q = (rms_norm(c_q, q_norm_g) @ w_uq).reshape(B, S, H, MLA_NOPE_DIM + MLA_ROPE_DIM).transpose(0, 2, 1, 3)
    kv = (rms_norm(c_kv, kv_norm_g) @ w_ukv).reshape(B, S, H, MLA_NOPE_DIM + MLA_V_DIM).transpose(0, 2, 1, 3)
    q_full = jnp.concatenate([q[..., :MLA_NOPE_DIM], rope(q[..., MLA_NOPE_DIM:], pos)], axis=-1)
    k_pe = jnp.broadcast_to(rope(k_rope[:, None], pos), (B, H, S, MLA_ROPE_DIM))
    k_full = jnp.concatenate([kv[..., :MLA_NOPE_DIM], k_pe], axis=-1)
    v = kv[..., MLA_NOPE_DIM:]
    o = causal_attention_blocks(q_full, k_full, v, (MLA_NOPE_DIM + MLA_ROPE_DIM) ** -0.5)
    return o.transpose(0, 2, 1, 3).reshape(B, S, H * MLA_V_DIM)

def sparse_latent_mixer(x, w_in, pe_k, pe_v, cmp_k1, cmp_k2, cmp_v1, cmp_v2,
                        q_norm_g, w_uq, kv_norm_g, w_ukv, w_out):
    q_nsa, kv_nsa, gates, c_q, c_kv, k_rope = jnp.split(x @ w_in, SPLIT0, axis=-1)
    o_nsa = nsa_attention(q_nsa, kv_nsa, gates, pe_k, pe_v, cmp_k1, cmp_k2, cmp_v1, cmp_v2)
    o_mla = mla_attention(c_q, c_kv, k_rope, q_norm_g, w_uq, kv_norm_g, w_ukv)
    return jnp.concatenate([o_nsa, o_mla], axis=-1) @ w_out

def moba_attention(q, k, v):
    B, H, S, dh = q.shape
    Lb = MOBA_BLOCK
    nb = -(-S // Lb)
    pad = ((0, 0), (0, 0), (0, nb * Lb - S), (0, 0))
    kb = jnp.pad(k, pad).reshape(B, H, nb, Lb, dh)
    vb = jnp.pad(v, pad).reshape(B, H, nb, Lb, dh)
    scale = dh ** -0.5
    pos = jnp.arange(S)
    n_top = min(MOBA_TOPK, max(nb - 1, 1))
    k_mean = jnp.mean(kb.astype(jnp.float32), axis=3).astype(k.dtype)
    gate = jnp.einsum('bhsd,bhnd->bhsn', q, k_mean).astype(jnp.float32)
    fully_past = jnp.arange(nb)[None, :] < (pos // Lb)[:, None]
    g_val, g_idx = lax.top_k(jnp.where(fully_past, gate, -jnp.inf), n_top)
    g_ok = g_val > -jnp.inf
    bi = jnp.arange(B)[:, None, None, None]
    hi = jnp.arange(H)[None, :, None, None]
    own_off = jnp.arange(Lb)

    def chunk(args):
        qb, qp, idx, ok = args
        qc = qb.shape[2]
        own = qp[0] // Lb
        k_own = lax.dynamic_index_in_dim(kb, own, axis=2, keepdims=False)
        v_own = lax.dynamic_index_in_dim(vb, own, axis=2, keepdims=False)
        kg = kb[bi, hi, idx].reshape(B, H, qc, n_top * Lb, dh)
        vg = vb[bi, hi, idx].reshape(B, H, qc, n_top * Lb, dh)
        s_past = jnp.einsum('bhqd,bhqkd->bhqk', qb, kg) * scale
        s_own = jnp.einsum('bhqd,bhkd->bhqk', qb, k_own) * scale
        m_own = jnp.broadcast_to((own * Lb + own_off)[None, :] <= qp[:, None], (B, H, qc, Lb))
        mask = jnp.concatenate([jnp.repeat(ok, Lb, axis=-1), m_own], axis=-1)
        p = masked_softmax(jnp.concatenate([s_past, s_own], axis=-1), mask).astype(v.dtype)
        return (jnp.einsum('bhqk,bhqkd->bhqd', p[..., :n_top * Lb], vg)
                + jnp.einsum('bhqk,bhkd->bhqd', p[..., n_top * Lb:], v_own))

    o = lax.map(chunk, (seq_blocks(q, 2, MOBA_Q_CHUNK), pos.reshape(-1, MOBA_Q_CHUNK),
                        seq_blocks(g_idx, 2, MOBA_Q_CHUNK), seq_blocks(g_ok, 2, MOBA_Q_CHUNK)))
    return merge_blocks(o, 2)

def moba_mixer(x, w_qkv, w_out):
    B, S, _ = x.shape
    pos = jnp.arange(S)
    q, k, v = [t.reshape(B, S, MOBA_HEADS, HEAD_DIM).transpose(0, 2, 1, 3)
               for t in jnp.split(x @ w_qkv, 3, axis=-1)]
    o = moba_attention(rope(q, pos), rope(k, pos), v)
    return o.transpose(0, 2, 1, 3).reshape(B, S, MOBA_HEADS * HEAD_DIM) @ w_out

def moe_ffn(x, w_router, router_bias, w_gate, w_up, w_down, ws_gate, ws_up, ws_down):
    B, S, D = x.shape
    T = B * S
    xt = x.reshape(T, D)
    scores = jax.nn.sigmoid((xt @ w_router).astype(jnp.float32))
    choice = scores + router_bias.astype(jnp.float32)
    grp_score = lax.top_k(choice.reshape(T, N_GROUPS, N_EXPERTS // N_GROUPS), 2)[0].sum(-1)
    _, g_idx = lax.top_k(grp_score, TOPK_GROUPS)
    g_mask = jnp.any(g_idx[:, :, None] == jnp.arange(N_GROUPS)[None, None, :], axis=1)
    e_mask = jnp.repeat(g_mask, N_EXPERTS // N_GROUPS, axis=1)
    _, e_idx = lax.top_k(jnp.where(e_mask, choice, -jnp.inf), TOP_K)
    w = jnp.take_along_axis(scores, e_idx, axis=-1)
    w = w / jnp.sum(w, axis=-1, keepdims=True) * ROUTED_SCALE

    A = T * TOP_K
    RB = MOE_ROW_BLOCK
    NB = -(-(A + N_EXPERTS * (RB - 1)) // RB)
    e_flat = e_idx.reshape(A)
    tok_flat = jnp.repeat(jnp.arange(T), TOP_K)
    order = jnp.argsort(e_flat)
    e_sorted = e_flat[order]
    counts = jnp.bincount(e_flat, length=N_EXPERTS)
    padded = (counts + RB - 1) // RB * RB
    start = jnp.cumsum(counts) - counts
    p_end = jnp.cumsum(padded)
    dest = (p_end - padded)[e_sorted] + jnp.arange(A) - start[e_sorted]
    row_tok = jnp.full((NB * RB,), T, jnp.int32).at[dest].set(tok_flat[order].astype(jnp.int32))
    row_gate = jnp.zeros((NB * RB,), x.dtype).at[dest].set(w.reshape(A)[order].astype(x.dtype))
    blk_expert = jnp.minimum(jnp.searchsorted(p_end, jnp.arange(NB) * RB, side='right'), N_EXPERTS - 1)
    x_pad = jnp.concatenate([xt, jnp.zeros((1, D), xt.dtype)], axis=0)

    def expert_block(args):
        tok, gate, e = args
        xb = x_pad[tok]
        h = jax.nn.silu(xb @ w_gate[e]) * (xb @ w_up[e])
        return (h @ w_down[e]) * gate[:, None]

    ys = lax.map(expert_block, (row_tok.reshape(NB, RB), row_gate.reshape(NB, RB), blk_expert))
    routed = jax.ops.segment_sum(ys.reshape(NB * RB, D), row_tok, num_segments=T + 1)[:T]
    shared = (jax.nn.silu(xt @ ws_gate) * (xt @ ws_up)) @ ws_down
    return (routed + shared).astype(x.dtype).reshape(B, S, D)

def _normal(key, shape, scale):
    return jax.random.normal(key, shape, jnp.float32) * scale

def setup_inputs(seed: int = 0) -> dict:
    key = jax.random.key(seed)
    k_x, k_layers = jax.random.split(key)
    out = {"x": jax.random.normal(k_x, (BATCH, SEQ, D_MODEL), jnp.float32)}
    for i, lk in enumerate(jax.random.split(k_layers, DEPTH)):
        ks = iter(jax.random.split(lk, 32))
        p = "l%d_" % i
        if i % 2 == 0:
            out[p + "w_in"] = _normal(next(ks), (D_MODEL, IN_W0), D_MODEL ** -0.5)
            out[p + "nsa_pe_k"] = _normal(next(ks), (NSA_CMP_LEN, HEAD_DIM), 0.1)
            out[p + "nsa_pe_v"] = _normal(next(ks), (NSA_CMP_LEN, HEAD_DIM), 0.1)
            out[p + "nsa_cmp_k1"] = _normal(next(ks), (NSA_CMP_LEN * HEAD_DIM, NSA_CMP_HIDDEN), (NSA_CMP_LEN * HEAD_DIM) ** -0.5)
            out[p + "nsa_cmp_k2"] = _normal(next(ks), (NSA_CMP_HIDDEN, HEAD_DIM), NSA_CMP_HIDDEN ** -0.5)
            out[p + "nsa_cmp_v1"] = _normal(next(ks), (NSA_CMP_LEN * HEAD_DIM, NSA_CMP_HIDDEN), (NSA_CMP_LEN * HEAD_DIM) ** -0.5)
            out[p + "nsa_cmp_v2"] = _normal(next(ks), (NSA_CMP_HIDDEN, HEAD_DIM), NSA_CMP_HIDDEN ** -0.5)
            out[p + "mla_q_norm"] = 1.0 + _normal(next(ks), (MLA_Q_RANK,), 0.01)
            out[p + "mla_w_uq"] = _normal(next(ks), (MLA_Q_RANK, MLA_HEADS * (MLA_NOPE_DIM + MLA_ROPE_DIM)), MLA_Q_RANK ** -0.5)
            out[p + "mla_kv_norm"] = 1.0 + _normal(next(ks), (MLA_KV_RANK,), 0.01)
            out[p + "mla_w_ukv"] = _normal(next(ks), (MLA_KV_RANK, MLA_HEADS * (MLA_NOPE_DIM + MLA_V_DIM)), MLA_KV_RANK ** -0.5)
            out[p + "w_out"] = _normal(next(ks), (MIX_W0, D_MODEL), MIX_W0 ** -0.5 * DN_BETA)
        else:
            out[p + "w_qkv"] = _normal(next(ks), (D_MODEL, 3 * MOBA_HEADS * HEAD_DIM), D_MODEL ** -0.5)
            out[p + "w_out"] = _normal(next(ks), (MOBA_HEADS * HEAD_DIM, D_MODEL), (MOBA_HEADS * HEAD_DIM) ** -0.5 * DN_BETA)
        out[p + "ln1_g"] = 1.0 + _normal(next(ks), (D_MODEL,), 0.01)
        out[p + "ln1_b"] = _normal(next(ks), (D_MODEL,), 0.01)
        out[p + "router"] = _normal(next(ks), (D_MODEL, N_EXPERTS), D_MODEL ** -0.5)
        out[p + "router_bias"] = _normal(next(ks), (N_EXPERTS,), 0.01)
        out[p + "exp_gate"] = _normal(next(ks), (N_EXPERTS, D_MODEL, EXPERT_FF), D_MODEL ** -0.5)
        out[p + "exp_up"] = _normal(next(ks), (N_EXPERTS, D_MODEL, EXPERT_FF), D_MODEL ** -0.5)
        out[p + "exp_down"] = _normal(next(ks), (N_EXPERTS, EXPERT_FF, D_MODEL), EXPERT_FF ** -0.5 * DN_BETA)
        out[p + "sh_gate"] = _normal(next(ks), (D_MODEL, SHARED_FF), D_MODEL ** -0.5)
        out[p + "sh_up"] = _normal(next(ks), (D_MODEL, SHARED_FF), D_MODEL ** -0.5)
        out[p + "sh_down"] = _normal(next(ks), (SHARED_FF, D_MODEL), SHARED_FF ** -0.5 * DN_BETA)
        out[p + "ln2_g"] = 1.0 + _normal(next(ks), (D_MODEL,), 0.01)
        out[p + "ln2_b"] = _normal(next(ks), (D_MODEL,), 0.01)
    return out

def reference(x,
              l0_w_in, l0_nsa_pe_k, l0_nsa_pe_v, l0_nsa_cmp_k1, l0_nsa_cmp_k2, l0_nsa_cmp_v1, l0_nsa_cmp_v2,
              l0_mla_q_norm, l0_mla_w_uq, l0_mla_kv_norm, l0_mla_w_ukv, l0_w_out,
              l0_ln1_g, l0_ln1_b, l0_router, l0_router_bias, l0_exp_gate, l0_exp_up, l0_exp_down,
              l0_sh_gate, l0_sh_up, l0_sh_down, l0_ln2_g, l0_ln2_b,
              l1_w_qkv, l1_w_out, l1_ln1_g, l1_ln1_b, l1_router, l1_router_bias,
              l1_exp_gate, l1_exp_up, l1_exp_down, l1_sh_gate, l1_sh_up, l1_sh_down, l1_ln2_g, l1_ln2_b):
    layers = [
        (lambda h: sparse_latent_mixer(h, l0_w_in, l0_nsa_pe_k, l0_nsa_pe_v, l0_nsa_cmp_k1, l0_nsa_cmp_k2,
                                       l0_nsa_cmp_v1, l0_nsa_cmp_v2, l0_mla_q_norm, l0_mla_w_uq,
                                       l0_mla_kv_norm, l0_mla_w_ukv, l0_w_out),
         (l0_ln1_g, l0_ln1_b),
         (l0_router, l0_router_bias, l0_exp_gate, l0_exp_up, l0_exp_down, l0_sh_gate, l0_sh_up, l0_sh_down),
         (l0_ln2_g, l0_ln2_b)),
        (lambda h: moba_mixer(h, l1_w_qkv, l1_w_out),
         (l1_ln1_g, l1_ln1_b),
         (l1_router, l1_router_bias, l1_exp_gate, l1_exp_up, l1_exp_down, l1_sh_gate, l1_sh_up, l1_sh_down),
         (l1_ln2_g, l1_ln2_b)),
    ]
    for i in range(DEPTH):
        mixer, ln1, moe_p, ln2 = layers[i]
        x = layer_norm(DN_ALPHA * x + mixer(x), *ln1)
        x = layer_norm(DN_ALPHA * x + moe_ffn(x, *moe_p), *ln2)
    return x


_drawn_inputs = setup_inputs


def setup_inputs(seed=0):
    import zlib

    import numpy as np

    out = dict(_drawn_inputs(seed))
    spreads = {}
    factors = {'l0_nsa_pe_k': 11.633,
     'l0_mla_q_norm': 8.0,
     'l0_mla_kv_norm': 6.568,
     'l0_ln2_b': 2.988,
     'l1_ln1_b': 2.959,
     'l1_ln2_g': 31.563,
     'l1_ln2_b': 32.67,
     'l0_nsa_pe_v': 2.726}
    for name, (base, spread) in spreads.items():
        noise = np.random.default_rng([zlib.crc32(name.encode()), seed]).standard_normal(out[name].shape)
        drawn = base * np.exp(spread * noise) if base else spread * noise
        out[name] = __import__('jax').numpy.asarray(drawn.astype(out[name].dtype))
    for name, factor in factors.items():
        out[name] = (out[name] * factor).astype(out[name].dtype)
    return out
```

```python
from contextlib import ExitStack

import numpy as np

import concourse.bass as bass
from concourse import mybir

F32 = mybir.dt.float32
BF16 = mybir.dt.bfloat16
I32 = mybir.dt.int32
ALU = mybir.AluOpType
ACT = mybir.ActivationFunctionType
AX = mybir.AxisListType

P = 128
T = 256
NT = T // P
D = 1024
KD = D // P
HD = 64
G, R = 2, 4
CMP_LEN, CMP_STRIDE = 32, 16
N_CMP = (T - CMP_LEN) // CMP_STRIDE + 1
NC = 16
QR, KVR, NOPE, ROPE_D = 256, 128, 64, 32
QK = NOPE + ROPE_D
W_IN = 1720
E_N, FF, TOPG = 64, 256, 4
PAIRS = E_N // 2
CAP = 64
RING = 4
SLOT = 2 * KD * FF + (FF // P) * D
CH = KD * 512
MR = 3
ALPHA = 4.0 ** 0.25
LN_EPS, RMS_EPS = 1e-5, 1e-6
NEG = -1e30
HIDE = -3e38

C_Q, C_KC, C_VC, C_KS, C_VS, C_KW, C_VW, C_GATE, C_CQ, C_CKV, C_KR = (
    0, 512, 640, 768, 896, 1024, 1152, 1280, 1304, 1560, 1688)
IN_CHUNKS = [(0, 512), (512, 512), (1024, 512), (1536, W_IN - 1536)]

CONST = {}
_at = 0
for _n, _w in (("ident", 128), ("before", 128), ("ones", 128), ("iota", CAP), ("lower", 64),
               ("rope64", NT * 2 * 64), ("rope32", NT * 2 * 32), ("ropec", 128), ("diag", 8), ("valid", NT)):
    CONST[_n] = (_at, _w)
    _at += _w
N_CONST = _at
N_MASK = 256 + NT * 128


def work_items(layer):
    quad = [(a, b) for a in range(NT) for b in range(2)]
    w = [("xT",) + q for q in quad]
    if layer == 0:
        w += [("proj", c, t) for c in range(4) for t in range(NT)]
        w += [("qT",) + q for q in quad] + [("kT", 0), ("kT", 1), ("kcvc",), ("hid", 0), ("hid", 1), ("cq",), ("ckv",),
                                            ("kcmp",), ("kcmpT",)]
        w += [("uq",) + q for q in quad] + [("ukv",) + q for q in quad]
        w += [("mqT",) + q for q in quad] + [("mkT",) + q for q in quad]
    else:
        for half in range(2):
            w += [("proj", half * 3 + c, t) for c in range(3) for t in range(NT)]
            w += [("qT", half) + q for q in quad] + [("kT", half) + q for q in quad]
    w += [("mixT",) + q for q in quad] + [("out",) + q for q in quad]
    w += [("yT",) + q for q in quad] + [("router",), ("rank",)]
    return w


WORK = {}
for _l in range(2):
    for _n in work_items(_l):
        WORK[(_l,) + _n] = len(WORK)

LAST_USE = [(0, "proj", c, 1) for c in range(4)] + [(0, "hid", 1), (0, "ukv", 1, 1), (0, "out", 0, 1), (0, "out", 1, 1),
                                                     (0, "router")]
LAST_USE += [(1, "proj", c, 1) for c in range(6)] + [(1, "out", 0, 1), (1, "out", 1, 1), (1, "router")]

GROUP = [(0, (0, 1, 2, 3)), (1, (0, 1)), (1, (2, 3)), (0, (4, 5, 6, 7)), (1, (4, 5)), (1, (6, 7))]
UNITS = {}
_u = 0
for _g in ("sel", "win", "cmp", "mla", "h0", "h1"):
    UNITS[_g] = _u
    _u += NT if _g == "cmp" else len(GROUP)


def build(nc, A, table, masks, peT, out):
    ctx = ExitStack()
    with ctx:
        def sb(name, shape, dt=F32):
            return ctx.enter_context(nc.sbuf_tensor(name, shape, dt))

        def sem(name):
            return ctx.enter_context(nc.semaphore(name))

        bank = [ctx.enter_context(nc.psum_tensor(f"bank{i}", [P, 512], F32)) for i in range(8)]
        work, s_bank, pt_bank, o_bank = bank[0:2], bank[2:4], bank[4:6], bank[6:8]

        ring = sb("ring", [P, RING, SLOT])
        mring = sb("mring", [P, MR, CH])
        x = sb("x", [P, NT, D])
        xT = sb("xT", [P, KD, T])
        mix = sb("mix", [P, NT, D])
        lnp = sb("lnp", [P, 2, D])
        cst = sb("cst", [P, N_CONST])
        identb = sb("identb", [P, P], BF16)
        maskb = sb("maskb", [P, N_MASK], BF16)
        kTn = sb("kTn", [64, 2, G, T])
        kfull = sb("kfull", [P, NT, 8, QK])
        p_sb = sb("p_sb", [P, 2, 512])
        pt_sb = sb("pt_sb", [P, 2, 512])
        tmp = sb("tmp", [P, 2, 512])
        pe_sb = sb("pe_sb", [P, CMP_LEN])
        negmax = sb("negmax", [P, 2, 8])
        rsum = sb("rsum", [P, NT, 8])
        wgt = sb("wgt", [P, NT, 8])
        gates = sb("gates", [P, NT, 24])
        stat = sb("stat", [P, NT, 12])
        mv = sb("mv", [P, NT, 2])
        var = sb("var", [P, 4])
        std = sb("std", [P, 4])
        rstd = sb("rstd", [P, 4])
        nwin_f = sb("nwin_f", [P, 4])
        krope = sb("krope", [P, NT, ROPE_D])
        nwin_i = sb("nwin_i", [P, 1], I32)

        scratch = ring[:, 2:4, :].rearrange("p a n -> p (a n)")

        def view(at, n):
            return scratch[:, at:at + n]
        proj = view(0, NT * W_IN).rearrange("p (t n) -> p t n", t=NT)
        proj1 = view(0, NT * 1024).rearrange("p (t n) -> p t n", t=NT)
        qT = view(3440, 2048).rearrange("p (h t) -> p h t", h=8)
        kT = view(5488, 2048).rearrange("p (h t) -> p h t", h=8)
        ukv = view(7536, 2048).rearrange("p (t n) -> p t n", t=NT)
        vmoba = view(7536, 2048).rearrange("p (a t n) -> p a t n", a=2, t=NT)
        qr = view(9584, 1024).rearrange("p (t n) -> p t n", t=NT)
        mlaq = view(10608, 1536).rearrange("p (t h n) -> p t h n", t=NT, h=8)
        kr = view(10608, 1024).rearrange("p (t n) -> p t n", t=NT)
        blocks = view(10608, 1024).rearrange("p (l g c) -> p l g c", l=CMP_LEN, g=G)

        def kv_pairs(t):
            return proj[:, t, C_KC:C_KC + 256].rearrange("p (g a d) -> p a g d", g=G, a=2)
        kr0 = p_sb[:, 1, :].rearrange("p (t n) -> p t n", t=NT)
        kcvcT = kT[:, 0:2, :]
        lat = kfull[:, :, :, :].rearrange("p t h n -> p (t h n)")[:, 0:768]
        cqn = lat[:, 0:512].rearrange("p (t n) -> p t n", t=NT)
        ckvn = lat[:, 512:768].rearrange("p (t n) -> p t n", t=NT)
        vbd = xT[:, 0:2, :].rearrange("p a n -> p (a n)").rearrange("p (h d) -> p h d", h=8)
        hx, hy, hz = (xT[:, 2 + i, 0:64] for i in range(3))
        hk = xT[:, 5, 0:64]
        kc = xT[0:32, 6, 0:64]
        kcr = xT[0:32, 6, 64:128]
        kcmpT = xT[0:64, 6, 128:160]
        vrep = xT[:, 7, 0:64]
        mixT = xT
        mflat = mix[:, :, :].rearrange("p t n -> p (t n)")
        y_sb = mflat[:, 0:1024]
        selb = mflat[:, 1024:1152].bitcast(BF16).rearrange("p (t c) -> p t c", t=NT)
        selg = mflat[:, 1152:1408].rearrange("p (t c) -> p t c", t=NT)
        sil = mflat[:, 1408:1664]
        h_sb = mflat[:, 1664:1920]
        xg = p_sb[:, :, :].rearrange("p a n -> p (a n)").rearrange("p (k c) -> p k c", k=KD)
        comb = pt_sb
        sil_sh = tmp[:, 0, :]
        h_sh = tmp[:, 1, :].rearrange("p (j t) -> p j t", j=2)
        xb = mring[:, 2, 1024:4096].bitcast(BF16).rearrange("p (a t d) -> p a t d", a=3, t=NT)
        rest = mix
        rout = kfull[:, :, :, :].rearrange("p t h n -> p (t h n)")

        def rt(i):
            return rout[:, i * 128:(i + 1) * 128]
        score, choice, masked, replaced, picked, gate_w, rank = (
            rt(i).rearrange("p (t e) -> p t e", t=NT) for i in range(7))
        best8 = rt(7).rearrange("p (g n) -> p g n", n=8)
        cmpA, cmpB = rt(8), rt(9)
        grp = rt(10)[:, 0:16]
        gmask = rt(10)[:, 16:32]
        pen = rt(10)[:, 32:48]
        top8 = rt(10)[:, 48:64]
        wsum = rt(10)[:, 64:68]
        ident = cst[:, CONST["ident"][0]:CONST["ident"][0] + P]

        def con(name):
            a, w = CONST[name]
            return cst[:, a:a + w]
        rope64 = con("rope64").rearrange("p (t s n) -> p t s n", t=NT, s=2)
        rope32 = con("rope32").rearrange("p (t s n) -> p t s n", t=NT, s=2)
        ropec = con("ropec")[0:32, :].rearrange("p (s n) -> p s n", s=2)

        def wg(s):
            return ring[:, s, 0:KD * FF].rearrange("p (k f) -> p k f", k=KD)

        def wu(s):
            return ring[:, s, KD * FF:2 * KD * FF].rearrange("p (k f) -> p k f", k=KD)

        def wgu(s):
            return ring[:, s, 0:2 * KD * FF].rearrange("p (m k f) -> p m k f", m=2, k=KD)

        def wd(s):
            return ring[:, s, 2 * KD * FF:SLOT].rearrange("p (j d) -> p j d", j=FF // P)

        const_in = sem("const_in")
        masks_cast = sem("masks_cast")
        chunk_in = [sem(f"chunk_in{i}") for i in range(MR)]
        ln_in = sem("ln_in")
        ln_used = sem("ln_used")
        work_full = [sem(f"work_full{i}") for i in range(2)]
        work_free = [sem(f"work_free{i}") for i in range(2)]
        x_ready = sem("x_ready")
        roped = sem("roped")
        s_scores = sem("s_scores")
        s_max = sem("s_max")
        s_exp = sem("s_exp")
        s_pt = sem("s_pt")
        s_ptcopy = sem("s_ptcopy")
        s_pv = sem("s_pv")
        s_ocopy = sem("s_ocopy")
        act_gate = sem("act_gate")
        act_std = sem("act_std")
        var_ready = sem("var_ready")
        act_hid = sem("act_hid")
        hid_in = sem("hid_in")
        sig_ready = sem("sig_ready")
        routed = sem("routed")
        picked_ready = sem("picked_ready")
        dve_chain = sem("dve_chain")
        act_chain = sem("act_chain")
        sh_gu = sem("sh_gu")
        sh_silu = sem("sh_silu")
        sh_h = sem("sh_h")
        part_ready = sem("part_ready")
        rest_ready = sem("rest_ready")
        experts_done = sem("experts_done")
        out_done = sem("out_done")
        L = [dict((n, sem(f"{n}_{l}")) for n in (
            "slot0", "slot1", "slot2", "slot3", "sel_ready", "xg_full", "xg_copied", "sel0_full", "sel0_copied",
            "ht_full", "ht_copied", "gu_full", "silu_done", "h_ready", "y_full", "y_copied", "window_done", "sel_chain",
            "rank_moved"))
             for l in range(2)]

        def value(stage):
            n = WORK[stage]
            return n % 2, n // 2

        block = ctx.enter_context(nc.Block())
        p_names = ("l0_", "l1_")

        ROPED = {}
        for i, n in enumerate(("q", "k", "kv_lat", "blocks", "cmpk", "vbd", "mlaq", "mlak", "q0", "k0", "q1", "k1")):
            ROPED[n] = i + 1

        @block.sync
        def _(sp):
            sp.dma_start(x[:, :, :], A["x"][0].rearrange("(t p) d -> p t d", p=P)).then_inc(const_in, 16)
            sp.dma_start(cst[:, :], table).then_inc(const_in, 16)
            sp.dma_start(scratch[:, 0:N_MASK], masks).then_inc(const_in, 16)
            sp.dma_start(pe_sb[:, :], peT).then_inc(const_in, 16)
            for l in range(2):
                S, pre = L[l], p_names[l]
                slot = [S[f"slot{i}"] for i in range(RING)]

                def load(s, g_src, u_src, d_src):
                    sp.dma_start(wg(s), g_src.rearrange("(p k) f -> p k f", k=KD)).then_inc(slot[s], 16)
                    sp.dma_start(wu(s), u_src.rearrange("(p k) f -> p k f", k=KD)).then_inc(slot[s], 16)
                    sp.dma_start(wd(s), d_src.rearrange("(j p) d -> p j d", p=P)).then_inc(slot[s], 16)

                def load_expert(s, e):
                    if isinstance(e, int):
                        load(s, A[pre + "exp_gate"][e], A[pre + "exp_up"][e], A[pre + "exp_down"][e])
                    else:
                        load(s, *(A[pre + n][bass.ds(e, 1)].rearrange("a k f -> (a k) f")
                                  for n in ("exp_gate", "exp_up", "exp_down")))

                if l == 0:
                    sp.wait_ge(chunk_in[2], 16)
                else:
                    sp.wait_ge(experts_done, 1)
                load(0, A[pre + "sh_gate"], A[pre + "sh_up"], A[pre + "sh_down"])
                load_expert(1, 0)
                for h in range(2):
                    b, v = value((l, "mixT", 1, h))
                    sp.wait_ge(work_free[b], v + 1)
                load_expert(2, 1)
                load_expert(3, 2)
                sp.wait_ge(routed, l + 1)
                windows = sp.value_load(nwin_i[0:1, 0:1], min_val=1, max_val=4)
                with sp.Fori(0, windows) as w:
                    with sp.Fori(0, 15) as i:
                        for j in range(4):
                            sp.wait_ge(S["y_full"], w * (2 * PAIRS) + i * 4 + (2 * ((j + 1) // 2) + 2))
                            load_expert(j, i * 4 + (j + 3))
                    sp.wait_ge(S["y_full"], w * (2 * PAIRS) + 2 * 31)
                    load_expert(0, E_N - 1)
                    with sp.If(w + 1 < windows):
                        for j in range(3):
                            sp.wait_ge(S["y_full"], w * (2 * PAIRS) + 2 * (32 + (j == 2)))
                            load_expert(j + 1, j)
            sp.wait_ge(x_ready, 4 * NT)
            sp.dma_start(out[0].rearrange("(t p) d -> p t d", p=P), x[:, :, :]).then_inc(out_done, 16)
            sp.wait_ge(out_done, 16)

        @block.gpsimd
        def _(pool):
            c = 0

            def next_chunk():
                nonlocal c
                if c >= MR:
                    b, v = value(LAST_USE[c - MR])
                    pool.wait_ge(work_full[b], v + 1)
                c += 1
                return (c - 1) % MR

            def columns(src, a, w):
                s = next_chunk()
                pool.dma_start(mring[:, s, 0:KD * w].rearrange("p (k n) -> p k n", k=KD),
                               src[:, a:a + w].rearrange("(p k) n -> p k n", k=KD)).then_inc(chunk_in[s], 16)

            def norm_params(l, which, n):
                if n:
                    pool.wait_ge(ln_used, n)
                for i, k in enumerate("gb"):
                    pool.dma_start(lnp[:, i, :], A[f"l{l}_ln{which}_{k}"].partition_broadcast(P)).then_inc(ln_in, 16)

            for l in range(2):
                pre = p_names[l]
                if l == 0:
                    for a, w in IN_CHUNKS:
                        columns(A[pre + "w_in"], a, w)
                    norm_params(0, 1, 0)
                    s = next_chunk()
                    for i, k in enumerate(("cmp_k1", "cmp_v1")):
                        pool.dma_start(mring[64 * i:64 * i + 64, s, :].rearrange("p (l n) -> p l n", n=P),
                                       A[pre + "nsa_" + k].rearrange("(l d) n -> d l n", d=HD)).then_inc(chunk_in[s], 16)
                    s = next_chunk()
                    m = mring[:, s, :]
                    pool.dma_start(m[:, 0:1536].rearrange("p (k n) -> p k n", k=2),
                                   A[pre + "mla_w_uq"].rearrange("(p k) n -> p k n", k=2)).then_inc(chunk_in[s], 16)
                    pool.dma_start(m[:, 1536:2560], A[pre + "mla_w_ukv"]).then_inc(chunk_in[s], 16)
                    pool.dma_start(m[:, 2560:2624], A[pre + "nsa_cmp_k2"]).then_inc(chunk_in[s], 16)
                    pool.dma_start(m[:, 2624:2688], A[pre + "nsa_cmp_v2"]).then_inc(chunk_in[s], 16)
                    pool.dma_start(m[:, 2688:2944], A[pre + "mla_q_norm"].partition_broadcast(P)).then_inc(chunk_in[s], 16)
                    pool.dma_start(m[:, 2944:3072], A[pre + "mla_kv_norm"].partition_broadcast(P)).then_inc(chunk_in[s], 16)
                else:
                    for n in range(6):
                        if n == 2:
                            pool.wait_ge(experts_done, 1)
                        columns(A[pre + "w_qkv"], (n % 3) * D + (n // 3) * 512, 512)
                    norm_params(1, 1, 2)
                for n in range(2):
                    columns(A[pre + "w_out"], n * 512, 512)
                s = next_chunk()
                pool.dma_start(mring[:, s, 0:512].rearrange("p (k n) -> p k n", k=KD),
                               A[pre + "router"].rearrange("(p k) n -> p k n", k=KD)).then_inc(chunk_in[s], 16)
                pool.dma_start(mring[:, s, 512:576], A[pre + "router_bias"].partition_broadcast(P)).then_inc(chunk_in[s], 16)
                norm_params(l, 2, 2 * l + 1)

        CHUNKS = [16] * 4 + [32, 96, 16, 16, 32] + [16] * 8 + [32]
        chunk_value = [sum(CHUNKS[i] for i in range(n % MR, n + 1, MR)) for n in range(len(CHUNKS))]

        def chunk_landed(eng, n):
            eng.wait_ge(chunk_in[n % MR], chunk_value[n])
            return mring[:, n % MR, :]

        @block.tensor
        def _(pe):
            mm = pe.matmul

            def open_work(stage):
                b, v = value(stage)
                if v:
                    pe.wait_ge(work_free[b], v)
                return work[b]

            def close_work(ins, stage):
                ins.then_inc(work_full[value(stage)[0]], 1)

            def copied(stage):
                b, v = value(stage)
                pe.wait_ge(work_free[b], v + 1)

            def transposed(l, name, src):
                for t in range(NT):
                    for kh in range(2):
                        w = open_work((l, name, t, kh))
                        for i in range(4):
                            ins = pe.transpose(w[:, i * P:(i + 1) * P], src[:, t, 4 * kh + i::KD], ident)
                        close_work(ins, (l, name, t, kh))

            def head_transposes(stages, src, width, needs=None):
                for t in range(NT):
                    for half in range(2):
                        w = open_work(stages + (t, half))
                        for i in range(4):
                            ins = pe.transpose(w[0:width, i * P:(i + 1) * P], src(t, 4 * half + i), ident)
                        close_work(ins, stages + (t, half))

            def product(l, name, n, src, chunk, width):
                m = chunk_landed(pe, chunk)[:, 0:KD * width].rearrange("p (k n) -> p k n", k=KD)
                for t in range(NT):
                    w = open_work((l, name, n, t))
                    for k in range(KD):
                        ins = mm(w[:, 0:width], src[:, k, t * P:(t + 1) * P], m[:, k, :],
                                 start=(k == 0), stop=(k == KD - 1))
                    close_work(ins, (l, name, n, t))

            def scores(u, mask, parts):
                s = s_bank[u % 2]
                if u >= 2:
                    pe.wait_ge(s_exp, u - 1)
                mm(s[:, 0:parts[-1][1]], identb[:, :], mask, start=True, stop=False, skip_group_check=True)
                for a, b, q, k in parts:
                    ins = mm(s[:, a:b], q, k, start=False, stop=(b == parts[-1][1]), skip_group_check=True)
                ins.then_inc(s_scores, 1)

            def unit_scores(u, qt, heads, q, k):
                nk = (qt + 1) * P
                mask = maskb[:, 128 - 128 * qt:256] if qt else maskb[:, 128:256]
                reps = len(heads)
                scores(u, mask.unsqueeze(1).broadcast_to([P, reps, nk]),
                       [(i * nk, (i + 1) * nk, q(h, qt), k(h, nk)) for i, h in enumerate(heads)])

            def unit_transposes(u, n):
                pe.wait_ge(s_exp, u + 1)
                if u >= 2:
                    pe.wait_ge(s_ptcopy, u - 1)
                for i in range(n):
                    ins = pe.transpose(pt_bank[u % 2][:, i * P:(i + 1) * P], p_sb[:, u % 2, i * P:(i + 1) * P], ident)
                ins.then_inc(s_pt, 1)

            def unit_values(u, qt, heads, v):
                pe.wait_ge(s_ptcopy, u + 1)
                for i, h in enumerate(heads):
                    for kb in range(qt + 1):
                        ins = mm(o_bank[qt][:, h * HD:(h + 1) * HD],
                                 pt_sb[:, u % 2, (i * (qt + 1) + kb) * P:(i * (qt + 1) + kb + 1) * P],
                                 v(h, kb), start=(kb == 0), stop=(kb == qt), skip_group_check=True)
                ins.then_inc(s_pv, 1)

            def attention(name, ocopies, q, k, v):
                u0 = UNITS[name]
                for n in range(len(GROUP) + 2):
                    if n < len(GROUP):
                        unit_scores(u0 + n, *GROUP[n], q, k)
                    if 1 <= n <= len(GROUP):
                        unit_transposes(u0 + n - 1, 4)
                    if n >= 2:
                        if n == 2 and ocopies:
                            pe.wait_ge(s_ocopy, ocopies)
                        unit_values(u0 + n - 2, *GROUP[n - 2], v)

            pe.wait_ge(const_in, 64)
            for l in range(2):
                S = L[l]
                if l:
                    pe.wait_ge(x_ready, 2 * NT)
                transposed(l, "xT", x)
                for t in range(NT):
                    for kh in range(2):
                        copied((l, "xT", t, kh))
                if l == 0:
                    for c, (a, w) in enumerate(IN_CHUNKS):
                        product(l, "proj", c, xT, c, w)
                    pe.wait_ge(roped, ROPED["q"])
                    head_transposes((0, "qT"), lambda t, h: qr[:, t, h * HD:(h + 1) * HD], HD)
                    pe.wait_ge(roped, ROPED["k"])
                    for kind in range(2):
                        w = open_work((0, "kT", kind))
                        for g in range(G):
                            for t in range(NT):
                                a = kind * P + g * HD
                                ins = pe.transpose(w[0:HD, g * T + t * P:g * T + (t + 1) * P], kr0[:, t, a:a + HD], ident)
                        close_work(ins, (0, "kT", kind))
                    w = open_work((0, "kcvc"))
                    copied((0, "proj", 1, 0))
                    copied((0, "proj", 1, 1))
                    for g in range(G):
                        for t in range(NT):
                            ins = pe.transpose(w[:, g * T + t * P:g * T + (t + 1) * P], proj[:, t, C_KC + g * P:C_KC + (g + 1) * P], ident)
                    close_work(ins, (0, "kcvc"))
                    for t in range(NT):
                        for h in range(2):
                            copied((0, "qT", t, h))
                    copied((0, "kT", 0))
                    copied((0, "proj", 2, 1))
                    pe.wait_ge(masks_cast, 1)

                    def q_nsa(h, qt):
                        return qT[0:HD, h, qt * P:(qt + 1) * P]
                    attention("sel", 0, q_nsa, lambda h, nk: kTn[:, 0, h // R, 0:nk],
                              lambda h, kb: proj[:, kb, C_VS + h // R * HD:C_VS + (h // R + 1) * HD])
                    m = chunk_landed(pe, 4)
                    pe.wait_ge(roped, ROPED["blocks"])
                    for kind in range(2):
                        w = open_work((0, "hid", kind))
                        for i in range(CMP_LEN):
                            a = 64 * kind
                            ins = mm(w[:, 0:32], m[a:a + 64, i * P:(i + 1) * P],
                                     blocks[a:a + 64, i].rearrange("p g c -> p (g c)"),
                                     start=(i == 0), stop=(i == CMP_LEN - 1))
                        close_work(ins, (0, "hid", kind))
                    pe.wait_ge(roped, ROPED["kv_lat"])
                    w = open_work((0, "cq"))
                    for k in range(2):
                        for t in range(NT):
                            ins = pe.transpose(w[:, k * T + t * P:k * T + (t + 1) * P], cqn[:, t, k::2], ident)
                    close_work(ins, (0, "cq"))
                    w = open_work((0, "ckv"))
                    for t in range(NT):
                        ins = pe.transpose(w[:, t * P:(t + 1) * P], ckvn[:, t, :], ident)
                    close_work(ins, (0, "ckv"))
                    copied((0, "kT", 1))
                    attention("win", NT, q_nsa, lambda h, nk: kTn[:, 1, h // R, 0:nk],
                              lambda h, kb: proj[:, kb, C_VW + h // R * HD:C_VW + (h // R + 1) * HD])
                    m = chunk_landed(pe, 5)
                    w = open_work((0, "kcmp"))
                    pe.wait_ge(hid_in, 1)
                    mm(w[0:32, 0:64], hk[:, 0:32], m[:, 2560:2624], start=True, stop=True)
                    ins = mm(w[:, 64:128], tmp[:, 0, 0:128], m[:, 2624:2688], start=True, stop=True)
                    close_work(ins, (0, "kcmp"))
                    w = open_work((0, "kcmpT"))
                    pe.wait_ge(roped, ROPED["cmpk"])
                    close_work(pe.transpose(w[0:64, 0:32], kcr, ident[0:32, 0:32]), (0, "kcmpT"))
                    copied((0, "cq"))
                    copied((0, "ckv"))
                    for t in range(NT):
                        for half in range(2):
                            w = open_work((0, "uq", t, half))
                            for k in range(2):
                                ins = mm(w[:, 0:384], mix[:, k, 512 + t * P:512 + (t + 1) * P],
                                         m[:, k * 768 + half * 384:k * 768 + (half + 1) * 384],
                                         start=(k == 0), stop=(k == 1))
                            close_work(ins, (0, "uq", t, half))
                    for t in range(NT):
                        for half in range(2):
                            w = open_work((0, "ukv", t, half))
                            ins = mm(w[:, :], mix[:, 0, 768 + t * P:768 + (t + 1) * P],
                                     m[:, 1536 + half * 512:1536 + (half + 1) * 512], start=True, stop=True)
                            close_work(ins, (0, "ukv", t, half))
                    copied((0, "kcmpT"))
                    u0 = UNITS["cmp"]
                    for qt in range(NT):
                        scores(u0 + qt, maskb[:, 256 + qt * P:256 + (qt + 1) * P],
                               [(h * NC, (h + 1) * NC, q_nsa(h, qt), kcmpT[:, (h // R) * NC:(h // R + 1) * NC])
                                for h in range(8)])
                    for qt in range(NT):
                        unit_transposes(u0 + qt, 1)
                    pe.wait_ge(roped, ROPED["vbd"])
                    pe.wait_ge(s_ocopy, 2 * NT)
                    for qt in range(NT):
                        pe.wait_ge(s_ptcopy, u0 + qt + 1)
                        mm(o_bank[qt][:, :], pt_sb[:, (u0 + qt) % 2, 0:P], vbd.rearrange("p h d -> p (h d)"),
                           start=True, stop=True).then_inc(s_pv, 1)
                    pe.wait_ge(roped, ROPED["mlaq"])
                    head_transposes((0, "mqT"), lambda t, h: mlaq[:, t, h, :], QK)
                    pe.wait_ge(roped, ROPED["mlak"])
                    head_transposes((0, "mkT"), lambda t, h: kfull[:, t, h, :], QK)
                    for t in range(NT):
                        for h in range(2):
                            copied((0, "mqT", t, h))
                            copied((0, "mkT", t, h))
                    attention("mla", 3 * NT, lambda h, qt: qT[0:QK, h, qt * P:(qt + 1) * P],
                              lambda h, nk: kT[0:QK, h, 0:nk],
                              lambda h, kb: ukv[:, kb, h * P + HD:(h + 1) * P])
                    chunk0 = 6
                    ocopies = 4 * NT
                else:
                    for half in range(2):
                        for c in range(3):
                            product(1, "proj", 3 * half + c, xT, 9 + 3 * half + c, 512)
                        pe.wait_ge(roped, ROPED[f"q{half}"])
                        head_transposes((1, "qT", half), lambda t, h: qr[:, t, h * HD:(h + 1) * HD], HD)
                        pe.wait_ge(roped, ROPED[f"k{half}"])
                        head_transposes((1, "kT", half), lambda t, h: kr[:, t, h * HD:(h + 1) * HD], HD)
                        for t in range(NT):
                            copied((1, "proj", 3 * half + 2, t))
                            for h in range(2):
                                copied((1, "qT", half, t, h))
                                copied((1, "kT", half, t, h))
                        attention(f"h{half}", (4 + half) * NT, lambda h, qt: qT[0:HD, h, qt * P:(qt + 1) * P],
                                  lambda h, nk: kT[0:HD, h, 0:nk],
                                  lambda h, kb, half=half: vmoba[:, half, kb, h * HD:(h + 1) * HD])
                    chunk0 = 15
                    ocopies = 6 * NT
                pe.wait_ge(s_ocopy, ocopies)
                transposed(l, "mixT", mix)
                for t in range(NT):
                    for kh in range(2):
                        copied((l, "mixT", t, kh))
                for n in range(2):
                    product(l, "out", n, mixT, chunk0 + n, 512)
                pe.wait_ge(x_ready, (2 * l + 1) * NT)
                transposed(l, "yT", x)
                for t in range(NT):
                    for kh in range(2):
                        copied((l, "yT", t, kh))
                m = chunk_landed(pe, chunk0 + 2)[:, 0:512].rearrange("p (k n) -> p k n", k=KD)
                w = open_work((l, "router"))
                for t in range(NT):
                    for k in range(KD):
                        ins = mm(w[:, t * E_N:(t + 1) * E_N], xT[:, k, t * P:(t + 1) * P], m[:, k, :],
                                 start=(k == 0), stop=(k == KD - 1))
                close_work(ins, (l, "router"))
                pe.wait_ge(S["slot0"], 48)
                for b, mat in enumerate((wg(0), wu(0))):
                    for j in range(2):
                        for k in range(KD):
                            ins = mm(s_bank[b][:, j * T:(j + 1) * T], mat[:, k, j * P:(j + 1) * P], xT[:, k, :],
                                     start=(k == 0), stop=(k == KD - 1))
                ins.then_inc(sh_gu, 1)
                w = open_work((l, "rank"))
                pe.wait_ge(picked_ready, l + 1)
                before, ones = con("before"), con("ones")
                mm(w[:, 0:64], before, picked[:, 0, :], start=True, stop=True)
                mm(w[:, 64:128], ones, picked[:, 0, :], start=True, stop=False)
                mm(w[:, 64:128], before, picked[:, 1, :], start=False, stop=True)
                mm(w[:, 128:192], ones, picked[:, 0, :], start=True, stop=False)
                close_work(mm(w[:, 128:192], ones, picked[:, 1, :], start=False, stop=True), (l, "rank"))
                pe.wait_ge(sh_h, l + 1)
                for j in range(2):
                    for t in range(NT):
                        for n in range(2):
                            ins = mm(bank[4 + 2 * t + n][:, :], h_sh[:, j, t * P:(t + 1) * P],
                                     wd(0)[:, j, n * 512:(n + 1) * 512], start=(j == 0), stop=False,
                                     skip_group_check=True)
                            if j == t == 1:
                                ins.then_inc(S["y_full"], 1)
                pe.wait_ge(routed, l + 1)
                copied((l, "rank"))
                pe.wait_ge(part_ready, 6 * (l + 1))
                windows = pe.value_load(nwin_i[0:1, 0:1], min_val=1, max_val=4)

                def gather(at, half):
                    if half == 0:
                        pe.wait_ge(S["sel_ready"], at + 1)
                    else:
                        pe.wait_ge(S["xg_copied"], at * 2 + 1)
                    for i in range(4):
                        n = 0
                        for t in range(NT):
                            for part in range(3):
                                ins = mm(bank[0][:, i * P:(i + 1) * P], xb[:, part, t, 4 * half + i::KD], selb[:, t, :],
                                         start=(n == 0), stop=(n == 5))
                                n += 1
                    ins.then_inc(S["xg_full"], 1)

                def turn_sel():
                    for t in range(NT):
                        ins = pe.transpose(bank[1][:, T + t * P:T + (t + 1) * P], selg[:, t, :], ident)
                    return ins

                def turn_h(at):
                    pe.wait_ge(S["h_ready"], at + 1)
                    for j in range(2):
                        ins = pe.transpose(bank[1][:, j * P:(j + 1) * P], h_sb[:, j * P:(j + 1) * P], ident)
                    return ins

                def gate_up(at, slots):
                    pe.wait_ge(S["xg_copied"], at * 2 + 2)
                    for s, v in slots:
                        pe.wait_ge(S[f"slot{s}"], v)
                    for k in range(KD):
                        for b, (s, _) in enumerate(slots):
                            ins = mm(bank[1][b * CAP:(b + 1) * CAP, :], xg[:, k, b * CAP:(b + 1) * CAP], wgu(s)[:, :, k, :],
                                     start=(k == 0), stop=(k == KD - 1))
                    ins.then_inc(S["gu_full"], 1)

                def down(at, slots, buf):
                    pe.wait_ge(S["ht_copied"], at + 1)
                    for n in range(2):
                        for j in range(2):
                            for b, (s, _) in enumerate(slots):
                                ins = mm(s_bank[n][b * CAP:(b + 1) * CAP, :], comb[:, buf, j * P + b * CAP:j * P + (b + 1) * CAP],
                                         wd(s)[:, j, n * 512:(n + 1) * 512], start=(j == 0), stop=(j == 1))
                        ins.then_inc(S["y_full"], 1)

                def scatter(at, buf):
                    pe.wait_ge(S["y_copied"], at * 2 + 2)
                    for t in range(NT):
                        for n in range(2):
                            ins = mm(bank[4 + 2 * t + n][:, :], comb[:, buf, T + t * P:T + (t + 1) * P],
                                     y_sb[:, n * 512:(n + 1) * 512], start=False, stop=False, skip_group_check=True)
                    return ins

                def pair(w, i, j, first=False, last=False):
                    at = w * PAIRS + i * 2 + j
                    v = w * (48 * E_N // RING) + i * 48
                    slots = ((3, v + 48), (0, v + 96)) if j else ((1, v + 48), (2, v + 48))
                    gate_up(at, slots)
                    if not last:
                        gather(at + 1, 0)
                    if not first:
                        scatter(at - 1, j)
                    ins = turn_h(at)
                    if not last:
                        ins = turn_sel()
                    ins.then_inc(S["ht_full"], 1)
                    if not last:
                        gather(at + 1, 1)
                    down(at, slots, j)

                with pe.Fori(0, windows) as w:
                    gather(w * PAIRS, 0)
                    turn_sel().then_inc(S["sel0_full"], 1)
                    gather(w * PAIRS, 1)
                    pe.wait_ge(S["sel0_copied"], w + 1)
                    for j in range(2):
                        pair(w, 0, j, first=(j == 0))
                    with pe.Fori(1, 15) as i:
                        for j in range(2):
                            pair(w, i, j)
                    for j in range(2):
                        pair(w, 15, j, last=(j == 1))
                    scatter(w * PAIRS + (PAIRS - 1), 0).then_inc(S["window_done"], 1)

        @block.scalar
        def _(act):
            cp = ACT.Copy

            def full(stage):
                b, v = value(stage)
                act.wait_ge(work_full[b], v + 1)
                return work[b]

            def free(ins, stage):
                ins.then_inc(work_free[value(stage)[0]], 1)

            def take(stage, dst, src=lambda w: w[:, :], scale=1.0):
                free(act.activation(dst, src(full(stage)), cp, scale=scale), stage)

            def exps(name, ngroup):
                u0 = UNITS[name]
                for n in range(ngroup):
                    u = u0 + n
                    act.wait_ge(s_max, u + 1)
                    if u >= 2:
                        act.wait_ge(s_pt, u - 1)
                    if name == "cmp":
                        ins = act.activation(p_sb[:, u % 2, 0:P], tmp[:, 1, n * P:(n + 1) * P], ACT.Exp)
                    else:
                        qt, heads = GROUP[n]
                        nk = (qt + 1) * P
                        for i, h in enumerate(heads):
                            ins = act.activation(p_sb[:, u % 2, i * nk:(i + 1) * nk], s_bank[u % 2][:, i * nk:(i + 1) * nk],
                                                 ACT.Exp, bias=negmax[:, u % 2, i:i + 1],
                                                 accum_out=rsum[:, qt, h:h + 1])
                    ins.then_inc(s_exp, 1)

            def wait_groups(n):
                act.wait_ge(s_ocopy, n)

            def roots(n, count):
                act.wait_ge(var_ready, n)
                act.activation(std[:, 0:count], var[:, 0:count], ACT.Sqrt).then_inc(act_std, 1)

            n_var = 0
            for l in range(2):
                S = L[l]
                for kh in range(2):
                    take((l, "xT", 0, kh), xT[:, 4 * kh:4 * kh + 4, 0:P], lambda w: w[:, :].rearrange("p (k n) -> p k n", k=4))
                if l == 0:
                    for c, (a, w) in enumerate(IN_CHUNKS):
                        if c == 0:
                            act.wait_ge(masks_cast, 1)
                            take((0, "proj", 0, 0), proj[:, 0, 0:512], scale=1.0)
                        elif c == 1:
                            act.activation(kv_pairs(0), full((0, "proj", 1, 0))[:, 0:256].rearrange("p (a g d) -> p a g d", a=2, g=G), cp)
                            take((0, "proj", 1, 0), proj[:, 0, C_KS:C_KW], lambda b: b[:, 256:512])
                        else:
                            take((0, "proj", c, 0), proj[:, 0, a:a + w], lambda b, w=w: b[:, 0:w])
                    n_var += 1
                    roots(n_var, 4)
                    for b in range(2):
                        bb, v = value((0, "proj", 2, b))
                        act.wait_ge(work_free[bb], v + 1)
                    act.activation(gates[:, :, :], proj[:, :, C_GATE:C_GATE + 24], ACT.Exp, scale=-1.0).then_inc(act_gate, 1)
                    for h in range(2):
                        take((0, "qT", 0, h), qT[0:64, 4 * h:4 * h + 4, 0:P],
                             lambda w: w[0:64, :].rearrange("p (h n) -> p h n", h=4), scale=HD ** -0.5)
                    take((0, "kT", 0), kTn[:, 0, :, :], lambda w: w[0:64, :].rearrange("p (g n) -> p g n", g=G))
                    take((0, "kT", 1), kTn[:, 1, :, :], lambda w: w[0:64, :].rearrange("p (g n) -> p g n", g=G))
                    exps("sel", 6)
                    act.wait_ge(act_hid, 1)
                    act.activation(hz, hy, ACT.Exp, scale=-2.0 * (2.0 / np.pi) ** 0.5).then_inc(act_gate, 1)
                    take((0, "cq"), mix[:, :, 512:768], lambda w: w[:, :].rearrange("p (k n) -> p k n", k=2))
                    take((0, "ckv"), mix[:, 0, 768:1024], lambda w: w[:, 0:T])
                    wait_groups(NT)
                    exps("win", 6)
                    for t in range(NT):
                        for half in range(2):
                            if t == 0:
                                take((0, "uq", t, half), mlaq[:, t, 4 * half:4 * half + 4, :],
                                     lambda w: w[:, 0:384].rearrange("p (h n) -> p h n", h=4), scale=QK ** -0.5)
                    for half in range(2):
                        take((0, "ukv", 0, half), ukv[:, 0, half * 512:(half + 1) * 512])
                    wait_groups(2 * NT)
                    exps("cmp", NT)
                    act.wait_ge(s_scores, UNITS["cmp"] + NT)
                    for h in range(2):
                        take((0, "mqT", 0, h), qT[0:QK, 4 * h:4 * h + 4, 0:P],
                             lambda w: w[0:QK, :].rearrange("p (h n) -> p h n", h=4))
                    for h in range(2):
                        take((0, "mkT", 0, h), kT[0:QK, 4 * h:4 * h + 4, 0:P],
                             lambda w: w[0:QK, :].rearrange("p (h n) -> p h n", h=4))
                    wait_groups(3 * NT)
                    exps("mla", 6)
                else:
                    for half in range(2):
                        for c in range(2):
                            take((1, "proj", 3 * half + c, 0), proj1[:, 0, c * 512:(c + 1) * 512])
                        take((1, "proj", 3 * half + 2, 0), vmoba[:, half, 0, :])
                        for h in range(2):
                            take((1, "qT", half, 0, h), qT[0:HD, 4 * h:4 * h + 4, 0:P],
                                 lambda w: w[0:HD, :].rearrange("p (h n) -> p h n", h=4), scale=HD ** -0.5)
                        for h in range(2):
                            take((1, "kT", half, 0, h), kT[0:HD, 4 * h:4 * h + 4, 0:P],
                                 lambda w: w[0:HD, :].rearrange("p (h n) -> p h n", h=4))
                        wait_groups((4 + half) * NT)
                        exps(f"h{half}", 6)
                for kh in range(2):
                    take((l, "mixT", 0, kh), mixT[:, 4 * kh:4 * kh + 4, 0:P],
                         lambda w: w[:, :].rearrange("p (k n) -> p k n", k=4))
                for t in range(NT):
                    n_var += 1
                    roots(n_var, 1)
                for kh in range(2):
                    take((l, "yT", 0, kh), xT[:, 4 * kh:4 * kh + 4, 0:P],
                         lambda w: w[:, :].rearrange("p (k n) -> p k n", k=4))
                chunk_landed(act, 8 + 9 * l)
                for part in range(3):
                    for t in range(NT):
                        if part:
                            act.wait_ge(rest_ready, 4 * l + (part - 1) * NT + t + 1)
                        act.activation(xb[:, part, t, :], (x, rest, rest)[part][:, t, :], cp).then_inc(part_ready, 1)
                w = full((l, "router"))
                act.activation(score, w[:, 0:128].rearrange("p (t e) -> p t e", t=NT), ACT.Exp, scale=-1.0).then_inc(sig_ready, 1)
                act.wait_ge(sh_gu, l + 1)
                act.activation(sil_sh, s_bank[0][:, :], ACT.Silu).then_inc(sh_silu, 1)
                act.wait_ge(routed, l + 1)
                windows = act.value_load(nwin_i[0:1, 0:1], min_val=1, max_val=4)

                def take_xg(at):
                    act.wait_ge(S["xg_full"], at * 2 + 1)
                    act.activation(xg[:, 0:4, :], bank[0][:, :].rearrange("p (k c) -> p k c", k=4), cp).then_inc(S["xg_copied"], 1)

                def silu(at):
                    act.wait_ge(S["gu_full"], at + 1)
                    act.activation(sil, bank[1][:, 0:FF], ACT.Silu).then_inc(S["silu_done"], 1)

                def take_y(at):
                    act.wait_ge(S["y_full"], at * 2 + 4)
                    act.activation(y_sb[:, 512:1024], s_bank[1][:, :], cp).then_inc(S["y_copied"], 1)

                def pair(w, i, j, last=False):
                    at = w * PAIRS + i * 2 + j
                    silu(at)
                    if not last:
                        take_xg(at + 1)
                    act.wait_ge(S["ht_full"], at + 1)
                    n = T if last else 2 * T
                    act.activation(comb[:, j, 0:n], bank[1][:, 0:n], cp).then_inc(S["ht_copied"], 1)
                    take_y(at)

                with act.Fori(0, windows) as w:
                    take_xg(w * PAIRS)
                    act.wait_ge(S["sel0_full"], w + 1)
                    act.activation(comb[:, 1, T:2 * T], bank[1][:, T:2 * T], cp).then_inc(S["sel0_copied"], 1)
                    with act.Fori(0, 15) as i:
                        for j in range(2):
                            pair(w, i, j)
                    for j in range(2):
                        pair(w, 15, j, last=(j == 1))
                for t in range(NT):
                    n_var += 1
                    roots(n_var, 1)

        @block.vector
        def _(dve):
            chain = 0
            n_std = n_ln = n_o = n_split = 0
            tt, ts, stt = dve.tensor_tensor, dve.tensor_scalar, dve.scalar_tensor_tensor

            def link(ins):
                nonlocal chain
                chain += 1
                ins.then_inc(dve_chain, 1)
                dve.wait_ge(dve_chain, chain)

            def full(stage):
                b, v = value(stage)
                dve.wait_ge(work_full[b], v + 1)
                return work[b]

            def copied(stage):
                b, v = value(stage)
                dve.wait_ge(work_free[b], v + 1)

            def free(ins, stage):
                ins.then_inc(work_free[value(stage)[0]], 1)

            def take(stage, dst, src=lambda w: w[:, :], scale=None):
                s = src(full(stage))
                free(dve.tensor_copy(dst, s) if scale is None else ts(dst, s, scale, None, ALU.mult), stage)

            def rope(dst, src, tab, nh, d):
                np_ = src.shape[0]
                h = d // 2
                a = tmp[0:np_, 0, 0:nh * d].rearrange("p (h n) -> p h n", h=nh)
                b = tmp[0:np_, 1, 0:nh * d].rearrange("p (h n) -> p h n", h=nh)

                def bc(v, n):
                    return v.unsqueeze(1).broadcast_to([np_, nh, n])
                tt(a, src, bc(tab[:, 0, :], d), ALU.mult)
                tt(b[:, :, 0:h], src[:, :, h:d], bc(tab[:, 1, 0:h], h), ALU.mult)
                link(tt(b[:, :, h:d], src[:, :, 0:h], bc(tab[:, 1, h:d], h), ALU.mult))
                return tt(dst, a, b, ALU.add)

            def heads(v, nh):
                return v.rearrange("p (h n) -> p h n", h=nh)

            def unit_max(name, n):
                u = UNITS[name] + n
                dve.wait_ge(s_scores, u + 1)
                qt, hs = GROUP[n]
                dve.tensor_reduce(negmax[:, u % 2, 0:len(hs)], heads(s_bank[u % 2][:, :], len(hs)), AX.X, ALU.max,
                                  negate=True).then_inc(s_max, 1)

            def unit_turn(u, w=512):
                dve.wait_ge(s_pt, u + 1)
                if u >= 2:
                    dve.wait_ge(s_pv, u - 1)
                dve.tensor_copy(pt_sb[:, u % 2, 0:w], pt_bank[u % 2][:, 0:w]).then_inc(s_ptcopy, 1)

            def attention(name, finish):
                u0 = UNITS[name]
                for n in range(len(GROUP) + 1):
                    if n < len(GROUP):
                        unit_max(name, n)
                    if n:
                        unit_turn(u0 + n - 1)
                dve.wait_ge(s_exp, u0 + 6)
                link(dve.reciprocal(wgt[:, :, :], rsum[:, :, :]))
                finish(u0 + 6)

            def take_o(upto, col, gate, first):
                nonlocal n_o
                if gate is not None:
                    link(tt(wgt[:, :, :], wgt[:, :, :], gates[:, :, gate * 8:gate * 8 + 8], ALU.mult))
                dve.wait_ge(s_pv, upto)
                for t in range(NT):
                    o = heads(o_bank[t][:, :], 8)
                    w = wgt[:, t, :].unsqueeze(2).broadcast_to([P, 8, HD])
                    m = heads(mix[:, t, col:col + 512], 8)
                    if first:
                        tt(m, o, w, ALU.mult).then_inc(s_ocopy, 1)
                    else:
                        a = heads(tmp[:, t, :], 8)
                        link(tt(a, o, w, ALU.mult))
                        tt(m, m, a, ALU.add).then_inc(s_ocopy, 1)
                n_o += NT
                dve.wait_ge(s_ocopy, n_o)


            def residual(t, n, src):
                xs = x[:, t, n * 512:(n + 1) * 512]
                return stt(xs, xs, ALPHA, src, ALU.mult, ALU.add)

            def layer_norm():
                nonlocal n_std, n_ln
                for t in range(NT):
                    for n in range(2):
                        ins = dve.bn_stats(stat[:, t, 6 * n:6 * n + 6], x[:, t, n * 512:(n + 1) * 512])
                    link(ins)
                    link(dve.bn_aggr(mv[:, t, :], stat[:, t, :]))
                    if n_std + t:
                        dve.wait_ge(act_std, n_std + t)
                    ts(var[:, 0:1], mv[:, t, 1:2], LN_EPS, None, ALU.add).then_inc(var_ready, 1)
                    dve.wait_ge(act_std, n_std + t + 1)
                    link(dve.reciprocal(rstd[:, 0:1], std[:, 0:1]))
                    link(ts(x[:, t, :], x[:, t, :], mv[:, t, 0:1], rstd[:, 0:1], ALU.subtract, ALU.mult))
                    if t == 0:
                        dve.wait_ge(ln_in, 32 * (n_ln + 1))
                    link(tt(x[:, t, :], x[:, t, :], lnp[:, 0, :], ALU.mult))
                    ins = tt(x[:, t, :], x[:, t, :], lnp[:, 1, :], ALU.add)
                    ins.then_inc(x_ready, 1)
                dve.wait_ge(x_ready, (n_ln + 1) * NT)
                dve.engine_nop().then_inc(ln_used, 1)
                n_std += NT
                n_ln += 1

            dve.wait_ge(const_in, 64)
            dve.tensor_copy(identb[:, :], ident)
            dve.tensor_copy(maskb[:, :], scratch[:, 0:N_MASK]).then_inc(masks_cast, 1)
            for l in range(2):
                S = L[l]
                for kh in range(2):
                    take((l, "xT", 1, kh), xT[:, 4 * kh:4 * kh + 4, P:T], lambda w: w[:, :].rearrange("p (k n) -> p k n", k=4))
                if l == 0:
                    dve.wait_ge(masks_cast, 1)
                    take((0, "proj", 0, 1), proj[:, 1, 0:512])
                    copied((0, "proj", 0, 0))
                    copied((0, "proj", 0, 1))
                    for t in range(NT):
                        ins = rope(heads(qr[:, t, :], 8), heads(proj[:, t, C_Q:C_Q + 512], 8), rope64[:, t], 8, HD)
                        link(ins)
                    dve.engine_nop().then_inc(roped, 1)
                    dve.tensor_copy(kv_pairs(1), full((0, "proj", 1, 1))[:, 0:256].rearrange("p (a g d) -> p a g d", a=2, g=G))
                    take((0, "proj", 1, 1), proj[:, 1, C_KS:C_KW], lambda b: b[:, 256:512])
                    take((0, "proj", 2, 1), proj[:, 1, 1024:1536])
                    take((0, "proj", 3, 1), proj[:, 1, 1536:W_IN], lambda b: b[:, 0:W_IN - 1536])
                    for c in range(1, 4):
                        copied((0, "proj", c, 0))
                        copied((0, "proj", c, 1))
                    for t in range(NT):
                        for i, a in enumerate((C_KS, C_KW)):
                            link(rope(heads(kr0[:, t, i * P:(i + 1) * P], 2), heads(proj[:, t, a:a + P], 2), rope64[:, t], 2, HD))
                    dve.engine_nop().then_inc(roped, 1)
                    for t in range(NT):
                        for i, (a, w) in enumerate(((C_CQ, QR), (C_CKV, KVR))):
                            link(dve.tensor_tensor_reduce(tmp[:, 0, 0:w], proj[:, t, a:a + w], proj[:, t, a:a + w], 1.0 / w,
                                                          RMS_EPS, ALU.mult, ALU.add, var[:, 2 * t + i:2 * t + i + 1]))
                    dve.engine_nop().then_inc(var_ready, 1)
                    dve.wait_ge(act_std, 1)
                    n_std = 1
                    link(dve.reciprocal(rstd[:, :], std[:, :]))
                    m5 = chunk_landed(dve, 5)
                    for t in range(NT):
                        for i, (a, w, g, dst) in enumerate(((C_CQ, QR, 2688, cqn), (C_CKV, KVR, 2944, ckvn))):
                            link(stt(dst[:, t, :], proj[:, t, a:a + w], rstd[:, 2 * t + i:2 * t + i + 1],
                                     m5[:, g:g + w], ALU.mult, ALU.mult))
                    dve.engine_nop().then_inc(roped, 1)
                    dve.wait_ge(act_gate, 1)
                    link(ts(gates[:, :, :], gates[:, :, :], 1.0, None, ALU.add))
                    link(dve.reciprocal(gates[:, :, :], gates[:, :, :]))
                    for h in range(2):
                        take((0, "qT", 1, h), qT[0:64, 4 * h:4 * h + 4, P:T],
                             lambda w: w[0:64, :].rearrange("p (h n) -> p h n", h=4), scale=HD ** -0.5)
                    take((0, "kcvc"), kcvcT, lambda w: w[:, :].rearrange("p (g n) -> p g n", g=G))
                    copied((0, "kcvc"))
                    link(dve.memset(blocks[:, :, :, N_CMP:NC], 0.0))
                    for g in range(G):
                        for hl in range(2):
                            a = kcvcT[:, g, hl * 16:hl * 16 + N_CMP * 16].rearrange("p (c l) -> p l c", l=16)
                            ins = tt(blocks[:, hl * 16:hl * 16 + 16, g, 0:N_CMP], a,
                                     pe_sb[:, hl * 16:hl * 16 + 16].unsqueeze(2).broadcast_to([P, 16, N_CMP]), ALU.add)
                            link(ins)
                    dve.engine_nop().then_inc(roped, 1)

                    def finish_first(col, gate, first):
                        return lambda upto: take_o(upto, col, gate, first)
                    attention("sel", finish_first(0, 1, True))
                    for kind in range(2):
                        take((0, "hid", kind), hx[:, 32 * kind:32 * kind + 32], lambda w: w[:, 0:32])
                    for kind in range(2):
                        copied((0, "hid", kind))
                    link(tt(hy, hx, hx, ALU.mult))
                    link(ts(hy, hy, 0.044715, 1.0, ALU.mult, ALU.add))
                    link(tt(hy, hy, hx, ALU.mult))
                    dve.engine_nop().then_inc(act_hid, 1)
                    dve.wait_ge(act_gate, 2)
                    link(ts(hz, hz, 1.0, None, ALU.add))
                    link(dve.reciprocal(hz, hz))
                    link(tt(hk, hx, hz, ALU.mult))
                    attention("win", finish_first(0, 2, False))
                    link(dve.tensor_copy(tmp[:, 0, 0:128].rearrange("p (g r c) -> p g r c", g=G, r=R),
                                    hk[:, 32:64].rearrange("p (g c) -> p g c", g=G).unsqueeze(2).broadcast_to([P, G, R, NC])))
                    dve.engine_nop().then_inc(hid_in, 1)
                    w = full((0, "kcmp"))
                    dve.tensor_copy(kc, w[0:32, 0:64])
                    free(dve.tensor_copy(vrep, w[:, 64:128]), (0, "kcmp"))
                    copied((0, "kcmp"))
                    link(rope(kcr.unsqueeze(1), kc.unsqueeze(1), ropec, 1, HD))
                    dve.engine_nop().then_inc(roped, 1)
                    link(tt(vbd, vrep.unsqueeze(1).broadcast_to([P, 8, HD]),
                            con("diag").unsqueeze(2).broadcast_to([P, 8, HD]), ALU.mult))
                    dve.engine_nop().then_inc(roped, 1)
                    take((0, "kcmpT"), kcmpT, lambda w: w[0:64, 0:32])
                    for half in range(2):
                        take((0, "uq", 1, half), mlaq[:, 1, 4 * half:4 * half + 4, :],
                             lambda w: w[:, 0:384].rearrange("p (h n) -> p h n", h=4), scale=QK ** -0.5)
                    for half in range(2):
                        take((0, "ukv", 1, half), ukv[:, 1, half * 512:(half + 1) * 512])
                    u0 = UNITS["cmp"]
                    for qt in range(NT):
                        dve.wait_ge(s_scores, u0 + qt + 1)
                        s = heads(s_bank[(u0 + qt) % 2][:, 0:P], 8)
                        link(dve.tensor_reduce(negmax[:, qt, 0:8], s, AX.X, ALU.max, negate=True))
                        tt(heads(tmp[:, 1, qt * P:(qt + 1) * P], 8), s, negmax[:, qt, 0:8].unsqueeze(2).broadcast_to([P, 8, NC]),
                           ALU.add).then_inc(s_max, 1)
                    for qt in range(NT):
                        dve.wait_ge(s_exp, u0 + qt + 1)
                        link(dve.tensor_reduce(rsum[:, qt, :], heads(p_sb[:, (u0 + qt) % 2, 0:P], 8), AX.X, ALU.add))
                    for qt in range(NT):
                        unit_turn(u0 + qt, P)
                    link(dve.reciprocal(wgt[:, :, :], rsum[:, :, :]))
                    link(tt(wgt[:, :, :], wgt[:, :, :], con("valid").unsqueeze(2).broadcast_to([P, NT, 8]), ALU.mult))
                    take_o(u0 + NT, 0, 0, False)
                    for t in range(NT):
                        for half in range(2):
                            copied((0, "uq", t, half))
                            copied((0, "ukv", t, half))
                    for t in range(NT):
                        q = mlaq[:, t, :, NOPE:QK]
                        link(rope(q, q, rope32[:, t], 8, ROPE_D))
                    dve.engine_nop().then_inc(roped, 1)
                    for t in range(NT):
                        kv = heads(ukv[:, t, :], 8)
                        dve.tensor_copy(kfull[:, t, :, 0:NOPE], kv[:, :, 0:NOPE])
                        link(rope(heads(krope[:, t, :], 1), heads(proj[:, t, C_KR:C_KR + ROPE_D], 1), rope32[:, t], 1, ROPE_D))
                        link(dve.tensor_copy(kfull[:, t, :, NOPE:QK],
                                             krope[:, t, :].unsqueeze(1).broadcast_to([P, 8, ROPE_D])))
                    dve.engine_nop().then_inc(roped, 1)
                    for h in range(2):
                        take((0, "mqT", 1, h), qT[0:QK, 4 * h:4 * h + 4, P:T],
                             lambda w: w[0:QK, :].rearrange("p (h n) -> p h n", h=4))
                    for h in range(2):
                        take((0, "mkT", 1, h), kT[0:QK, 4 * h:4 * h + 4, P:T],
                             lambda w: w[0:QK, :].rearrange("p (h n) -> p h n", h=4))
                    attention("mla", finish_first(512, None, True))
                else:
                    for half in range(2):
                        if half:
                            pass
                        for c in range(2):
                            take((1, "proj", 3 * half + c, 1), proj1[:, 1, c * 512:(c + 1) * 512])
                            copied((1, "proj", 3 * half + c, 0))
                            copied((1, "proj", 3 * half + c, 1))
                            for t in range(NT):
                                dst = (qr, kr)[c]
                                link(rope(heads(dst[:, t, :], 8), heads(proj1[:, t, c * 512:(c + 1) * 512], 8), rope64[:, t], 8, HD))
                            dve.engine_nop().then_inc(roped, 1)
                        take((1, "proj", 3 * half + 2, 1), vmoba[:, half, 1, :])
                        for h in range(2):
                            take((1, "qT", half, 1, h), qT[0:HD, 4 * h:4 * h + 4, P:T],
                                 lambda w: w[0:HD, :].rearrange("p (h n) -> p h n", h=4), scale=HD ** -0.5)
                        for h in range(2):
                            take((1, "kT", half, 1, h), kT[0:HD, 4 * h:4 * h + 4, P:T],
                                 lambda w: w[0:HD, :].rearrange("p (h n) -> p h n", h=4))
                        attention(f"h{half}", lambda upto, half=half: take_o(upto, half * 512, None, True))
                for kh in range(2):
                    take((l, "mixT", 1, kh), mixT[:, 4 * kh:4 * kh + 4, P:T],
                         lambda w: w[:, :].rearrange("p (k n) -> p k n", k=4))

                for n in range(2):
                    for t in range(NT):
                        free(residual(t, n, full((l, "out", n, t))[:, :]), (l, "out", n, t))
                for n in range(2):
                    for t in range(NT):
                        copied((l, "out", n, t))
                layer_norm()
                for kh in range(2):
                    take((l, "yT", 1, kh), xT[:, 4 * kh:4 * kh + 4, P:T],
                         lambda w: w[:, :].rearrange("p (k n) -> p k n", k=4))
                for part in range(2):
                    for t in range(NT):
                        n_split += 1
                        dve.wait_ge(part_ready, n_split + NT * l)
                        tt(rest[:, t, :], (x, rest)[part][:, t, :], xb[:, part, t, :], ALU.subtract).then_inc(rest_ready, 1)
                dve.wait_ge(sig_ready, l + 1)
                link(ts(score, score, 1.0, None, ALU.add))
                ins = dve.reciprocal(score, score)
                free(ins, (l, "router"))
                copied((l, "router"))
                bias = chunk_landed(dve, 8 + 9 * l)[:, 512:576]
                link(tt(choice, score, bias.unsqueeze(1).broadcast_to([P, NT, E_N]), ALU.add))
                flat = choice.rearrange("p t (g n) -> p (t g) n", n=8)
                for i in range(16):
                    ins = dve.max(best8[:, i, :], flat[:, i, :])
                link(ins)
                gs = grp.rearrange("p (t g) -> p t g", t=NT)
                link(tt(grp, best8[:, :, 0], best8[:, :, 1], ALU.add))
                other = gs.unsqueeze(2).broadcast_to([P, NT, 8, 8])
                own = gs.unsqueeze(3).broadcast_to([P, NT, 8, 8])
                a4 = cmpA.rearrange("p (t i j) -> p t i j", t=NT, i=8)
                b4 = cmpB.rearrange("p (t i j) -> p t i j", t=NT, i=8)
                link(tt(b4, other, own, ALU.is_equal))
                link(tt(cmpB.rearrange("p (t n) -> p t n", t=NT), cmpB.rearrange("p (t n) -> p t n", t=NT),
                        con("lower").unsqueeze(1).broadcast_to([P, NT, 64]), ALU.mult))
                link(tt(a4, other, own, ALU.is_gt))
                link(tt(cmpA, cmpA, cmpB, ALU.add))
                link(dve.tensor_reduce(gmask, cmpA.rearrange("p (g j) -> p g j", j=8), AX.X, ALU.add))
                link(ts(gmask, gmask, TOPG - 0.5, None, ALU.is_lt))
                ts(pen, gmask, -NEG, NEG, ALU.mult, ALU.add)
                mf = masked.rearrange("p t (g n) -> p (t g) n", n=8)
                link(tt(mf, flat, gmask.unsqueeze(2).broadcast_to([P, 16, 8]), ALU.mult))
                link(tt(mf, mf, pen.unsqueeze(2).broadcast_to([P, 16, 8]), ALU.add))
                for t in range(NT):
                    link(dve.max(top8[:, 8 * t:8 * t + 8], masked[:, t, :]))
                    link(dve.match_replace(replaced[:, t, :], top8[:, 8 * t:8 * t + 8], masked[:, t, :], HIDE))
                link(ts(picked, replaced, HIDE, None, ALU.is_equal))
                dve.engine_nop().then_inc(picked_ready, 1)
                link(tt(gate_w, score, picked, ALU.mult))
                link(dve.tensor_reduce(wsum[:, 0:2], gate_w, AX.X, ALU.add))
                link(dve.reciprocal(wsum[:, 2:4], wsum[:, 0:2]))
                for t in range(NT):
                    link(ts(gate_w[:, t, :], gate_w[:, t, :], wsum[:, 2 + t:3 + t], 2.5, ALU.mult, ALU.mult))
                dve.wait_ge(sh_silu, l + 1)
                tt(h_sh.rearrange("p j t -> p (j t)"), s_bank[1][:, :], sil_sh, ALU.mult).then_inc(sh_h, 1)
                w = full((l, "rank"))
                r2 = w[:, 0:128].rearrange("p (t e) -> p t e", t=NT)
                link(stt(rank, r2, 1000.0, picked, ALU.add, ALU.mult))
                link(ts(rank, rank, -1000.0, None, ALU.add))
                link(dve.tensor_reduce(nwin_f[:, 0:1], w[:, 128:192], AX.X, ALU.max))
                link(ts(nwin_f[:, 1:2], nwin_f[:, 0:1], float(CAP), 1.0, ALU.is_gt, ALU.add))
                link(stt(nwin_f[:, 2:3], nwin_f[:, 0:1], 2.0 * CAP, nwin_f[:, 1:2], ALU.is_gt, ALU.add))
                ins = stt(nwin_i[:, :], nwin_f[:, 0:1], 3.0 * CAP, nwin_f[:, 2:3], ALU.is_gt, ALU.add)
                free(ins, (l, "rank"))
                copied((l, "rank"))
                dve.engine_nop().then_inc(routed, 1)
                windows = dve.value_load(nwin_i[0:1, 0:1], min_val=1, max_val=4)

                def make_sel(pair0):
                    shape = [P, NT, 2, CAP]
                    two = bass.ds(pair0 * 2, 2)
                    iota = con("iota").unsqueeze(1).unsqueeze(1).broadcast_to(shape)
                    b4 = selb.rearrange("p t (b c) -> p t b c", b=2)
                    tt(b4, iota, rank[:, :, two].unsqueeze(3).broadcast_to(shape), ALU.is_equal).then_inc(S["sel_chain"], 1)
                    return b4, gate_w[:, :, two].unsqueeze(3).broadcast_to(shape)

                def make_gated(made, at):
                    dve.wait_ge(S["sel_chain"], at + 1)
                    tt(selg.rearrange("p t (b c) -> p t b c", b=2), made[0], made[1], ALU.mult).then_inc(S["sel_ready"], 1)

                def multiply(at):
                    dve.wait_ge(S["silu_done"], at + 1)
                    tt(h_sb, bank[1][:, FF:2 * FF], sil, ALU.mult).then_inc(S["h_ready"], 1)

                def take_xg(at):
                    dve.wait_ge(S["xg_full"], at * 2 + 2)
                    dve.tensor_copy(xg[:, 4:8, :], bank[0][:, :].rearrange("p (k c) -> p k c", k=4)).then_inc(S["xg_copied"], 1)

                def take_y(at):
                    dve.wait_ge(S["y_full"], at * 2 + 3)
                    dve.tensor_copy(y_sb[:, 0:512], s_bank[0][:, :]).then_inc(S["y_copied"], 1)

                def pair(w, i, j, ahead=2):
                    at = w * PAIRS + i * 2 + j
                    multiply(at)
                    if ahead:
                        take_xg(at + 1)
                    if ahead == 2:
                        make_gated(make_sel(i * 2 + (j + 2)), at + 2)
                    take_y(at)

                with dve.Fori(0, windows) as w:
                    make_gated(make_sel(0), w * PAIRS)
                    take_xg(w * PAIRS)
                    make_gated(make_sel(1), w * PAIRS + 1)
                    with dve.Fori(0, 15) as i:
                        for j in range(2):
                            pair(w, i, j)
                    for j in range(2):
                        pair(w, 15, j, ahead=1 - j)
                    ts(rank, rank, -float(CAP), None, ALU.add).then_inc(S["rank_moved"], 1)
                    dve.wait_ge(S["rank_moved"], w + 1)
                    dve.wait_ge(S["window_done"], w + 1)
                dve.engine_nop().then_inc(experts_done, 1)
                for t in range(NT):
                    for n in range(2):
                        ins = residual(t, n, bank[4 + 2 * t + n][:, :])
                link(ins)
                layer_norm()


_INS = ["x"] + ["l0_" + n for n in (
    "w_in", "nsa_cmp_k1", "nsa_cmp_k2", "nsa_cmp_v1", "nsa_cmp_v2", "mla_q_norm", "mla_w_uq", "mla_kv_norm",
    "mla_w_ukv")] + ["l1_w_qkv"] + [f"l{l}_{n}" for l in range(2) for n in (
        "w_out", "ln1_g", "ln1_b", "router", "router_bias", "exp_gate", "exp_up", "exp_down", "sh_gate", "sh_up",
        "sh_down", "ln2_g", "ln2_b")]


def rope_table(pos, d):
    half = d // 2
    inv = (np.float32(10000.0) ** (-np.arange(half, dtype=np.float32) / np.float32(half))).astype(np.float32)
    ang = (pos.astype(np.float32)[:, None] * inv[None, :]).astype(np.float64)
    c, s = np.cos(ang), np.sin(ang)
    return np.stack([np.concatenate([c, c], -1), np.concatenate([-s, s], -1)], 1).astype(np.float32)


def constants():
    p = np.arange(P)
    f = {"ident": np.eye(P), "before": (p[:, None] < p[None, :]), "ones": np.ones((P, P)),
         "iota": np.tile(np.arange(CAP), (P, 1)),
         "lower": np.tile((np.arange(8)[None, :] < np.arange(8)[:, None]).reshape(1, 64), (P, 1)),
         "diag": (p[:, None] // NC == np.arange(8)[None, :]),
         "valid": (p[:, None] + P * np.arange(NT)[None, :] >= CMP_LEN - 1)}
    for d in (64, 32):
        f[f"rope{d}"] = np.concatenate([rope_table(t * P + p, d).reshape(P, 2 * d) for t in range(NT)], 1)
    ends = np.tile(np.arange(NC) * CMP_STRIDE + CMP_LEN - 1, G)
    f["ropec"] = np.concatenate([rope_table(ends, 64).reshape(32, 128), np.zeros((P - 32, 128))], 0)
    tab = np.zeros((P, N_CONST), np.float32)
    for n, (a, w) in CONST.items():
        tab[:, a:a + w] = f[n]
    mask = np.zeros((P, N_MASK), np.float32)
    mask[:, 128:256] = np.where(p[None, :] > p[:, None], NEG, 0.0)
    c = p % NC
    for qt in range(NT):
        seen = (c[None, :] * CMP_STRIDE + CMP_LEN - 1 <= qt * P + p[:, None]) & (c[None, :] < N_CMP)
        mask[:, 256 + qt * P:256 + (qt + 1) * P] = np.where(seen, 0.0, NEG)
    return tab, mask


def kernel(**inputs):
    import concourse.bacc as _bacc
    from concourse import mybir as _mybir
    from concourse.bass_utils import run_bass_kernel_spmd as _run

    nc = _bacc.Bacc("TRN2", target_bir_lowering=False, num_devices=1)
    arrays, A = {}, {}

    def declare(name, a):
        a = np.ascontiguousarray(a)
        arrays[f"in_{name}_dram"] = a
        return nc.dram_tensor(f"in_{name}_dram", a.shape, _mybir.dt.from_np(a.dtype), kind="ExternalInput").ap()

    for name in _INS:
        A[name] = declare(name, inputs[name])
    peT = declare("peT", np.concatenate([np.asarray(inputs["l0_nsa_pe_k"]).T, np.asarray(inputs["l0_nsa_pe_v"]).T], 0))
    tab, mask = constants()
    table, masks = declare("table", tab), declare("masks", mask)
    out = nc.dram_tensor("out_0_dram", (1, T, D), _mybir.dt.from_np(np.dtype("float32")), kind="ExternalOutput").ap()
    build(nc, A, table, masks, peT, out)
    r = _run(nc, [arrays], core_ids=[0])
    return r.results[0]["out_0_dram"]
```

```python
from contextlib import ExitStack

import numpy as np

import concourse.bass as bass
from concourse import mybir

F32 = mybir.dt.float32
BF16 = mybir.dt.bfloat16
I32 = mybir.dt.int32
ALU = mybir.AluOpType
ACT = mybir.ActivationFunctionType
AX = mybir.AxisListType

P = 128
T = 256
NT = T // P
D = 1024
KD = D // P
HD = 64
G, R = 2, 4
CMP_LEN, CMP_STRIDE = 32, 16
N_CMP = (T - CMP_LEN) // CMP_STRIDE + 1
NC = 16
QR, KVR, NOPE, ROPE_D = 256, 128, 64, 32
QK = NOPE + ROPE_D
W_IN = 1720
E_N, FF, TOPG = 64, 256, 4
PAIRS = E_N // 2
CAP = 64
RING = 4
SLOT = 2 * KD * FF + (FF // P) * D
CH = KD * 512
MR = 3
ALPHA = 4.0 ** 0.25
LN_EPS, RMS_EPS = 1e-5, 1e-6
NEG = -1e30
HIDE = -3e38

C_Q, C_KC, C_VC, C_KS, C_VS, C_KW, C_VW, C_GATE, C_CQ, C_CKV, C_KR = (
    0, 512, 640, 768, 896, 1024, 1152, 1280, 1304, 1560, 1688)
IN_CHUNKS = [(0, 512), (512, 512), (1024, 512), (1536, W_IN - 1536)]

CONST = {}
_at = 0
for _n, _w in (("ident", 128), ("alpha", 128), ("before", 128), ("ones", 128), ("iota", CAP), ("lower", 64),
               ("rope64", NT * 2 * 64), ("rope32", NT * 2 * 32), ("ropec", 128), ("diag", 8), ("valid", NT)):
    CONST[_n] = (_at, _w)
    _at += _w
N_CONST = _at
N_MASK = 256 + NT * 128


def work_items(layer):
    quad = [(a, b) for a in range(NT) for b in range(2)]
    w = [("xT",) + q for q in quad]
    if layer == 0:
        proj = [[("proj", c, t) for t in range(NT)] for c in range(4)]
        w += proj[0] + proj[1] + [("qT",) + q for q in quad] + [("kcvc",)]
        w += proj[2] + [("kT", 0)] + proj[3] + [("kT", 1), ("hid",)]
        w += [("cq",), ("ckv",), ("hkT",), ("kcmp",), ("kcmpT",)]
        w += [("uq",) + q for q in quad] + [("ukv",) + q for q in quad]
        w += [("mkT",) + q for q in quad] + [("mqT",) + q for q in quad]
    else:
        for half in range(2):
            q, k, v = [[("proj", half * 3 + c, t) for t in range(NT)] for c in range(3)]
            w += q + k + v + [("qT", half) + z for z in quad] + [("kT", half) + z for z in quad]
    w += [("out", n, t) for t in range(NT) for n in range(2)]
    w += [("yT",) + q for q in quad] + [("router",), ("rank",)]
    return w


WORK = {}
for _l in range(2):
    for _n in work_items(_l):
        WORK[(_l,) + _n] = len(WORK)

LAST_USE = [(0, "proj", c, 1) for c in range(4)] + [(0, "hid"), (0, "ukv", 1, 1), (0, "out", 0, 1), (0, "out", 1, 1),
                                                     (0, "router")]
LAST_USE += [(1, "proj", c, 1) for c in range(6)] + [(1, "out", 0, 1), (1, "out", 1, 1), (1, "router")]

GROUP = [(0, (0, 1, 2, 3)), (1, (0, 1)), (1, (2, 3)), (0, (4, 5, 6, 7)), (1, (4, 5)), (1, (6, 7))]
UNITS = {}
_u = 0
for _g in ("sel", "win", "cmp", "mla", "h0", "h1"):
    UNITS[_g] = _u
    _u += NT if _g == "cmp" else len(GROUP)
CHAINS = [[(_g, _n) for _g in _gs for _n in range(NT if _g == "cmp" else len(GROUP))]
          for _gs in (("sel", "win", "cmp", "mla"), ("h0", "h1"))]
SUMS = {"cmp": 0, "mla": 4, "h0": 0, "h1": 4}
OPENS = ("sel", "mla", "h0", "h1")
NP = 4


def build(nc, A, table, masks, peT, out):
    ctx = ExitStack()
    with ctx:
        def sb(name, shape, dt=F32):
            return ctx.enter_context(nc.sbuf_tensor(name, shape, dt))

        def sem(name):
            return ctx.enter_context(nc.semaphore(name))

        bank = [ctx.enter_context(nc.psum_tensor(f"bank{i}", [P, 512], F32)) for i in range(8)]
        work, s_bank, pt_bank, o_bank = bank[0:2], bank[2:4], bank[4:6], bank[6:8]

        ring = sb("ring", [P, RING, SLOT])
        mring = sb("mring", [P, MR, CH])
        x = sb("x", [P, NT, D])
        xT = sb("xT", [P, KD, T])
        mix = sb("mix", [P, NT, D])
        lnp = sb("lnp", [P, 2, D])
        cst = sb("cst", [P, N_CONST])
        identb = sb("identb", [P, P], BF16)
        maskb = sb("maskb", [P, N_MASK], BF16)
        kTn = sb("kTn", [64, 2, G, T])
        kfull = sb("kfull", [P, NT, 8, QK])
        p_sb = sb("p_sb", [P, 2, 512])
        pt_sb = sb("pt_sb", [P, 2, 512])
        tmp = sb("tmp", [P, 2, 512])
        pe_sb = sb("pe_sb", [P, CMP_LEN])
        negmax = sb("negmax", [P, 2, 8])
        rsum = sb("rsum", [P, NT, 8])
        wgt = sb("wgt", [P, NT, 8])
        gates = sb("gates", [P, NT, 24])
        stat = sb("stat", [P, NT, 12])
        mv = sb("mv", [P, NT, 2])
        var = sb("var", [P, 4])
        std = sb("std", [P, 4])
        rstd = sb("rstd", [P, 4])
        nwin_f = sb("nwin_f", [P, 4])
        krope = sb("krope", [P, NT, ROPE_D])
        nwin_i = sb("nwin_i", [P, 1], I32)
        gate_of = sb("gate_of", [P, 2])

        scratch = ring[:, 2:4, :].rearrange("p a n -> p (a n)")

        def view(at, n):
            return scratch[:, at:at + n]
        proj = view(0, NT * W_IN).rearrange("p (t n) -> p t n", t=NT)
        qT = view(3440, 2048).rearrange("p (h t) -> p h t", h=8)
        kT = view(5488, 2048).rearrange("p (h t) -> p h t", h=8)
        ukv = view(7536, 2048).rearrange("p (t n) -> p t n", t=NT)
        blocks = view(7536, 2048).rearrange("p (l a g c) -> p l a g c", l=CMP_LEN, a=2, g=G)
        qr = view(9584, 1024).rearrange("p (t n) -> p t n", t=NT)
        mlaq = view(10608, 1536).rearrange("p (t h n) -> p t h n", t=NT, h=8)
        qTh = [view(1024 + 2048 * i, 2048).rearrange("p (h t) -> p h t", h=8) for i in range(2)]
        kTh = [view(5120 + 2048 * i, 2048).rearrange("p (h t) -> p h t", h=8) for i in range(2)]
        vmoba = view(9216, 2048).rearrange("p (a t n) -> p a t n", a=2, t=NT)
        qr1 = view(11264, 1024).rearrange("p (t n) -> p t n", t=NT)
        kr1 = kfull[:, :, :, :].rearrange("p t h n -> p (t h n)")[:, 0:1024].rearrange("p (t n) -> p t n", t=NT)

        def p_of(u):
            if u % NP < 2:
                return p_sb[:, u % NP, :]
            at = (9584 if u < UNITS["h0"] else 0) + 512 * (u % NP - 2)
            return view(at, 512)

        def kv_pairs(t):
            return proj[:, t, C_KC:C_KC + 256].rearrange("p (g a d) -> p a g d", g=G, a=2)
        kr0 = p_sb[:, 1, :].rearrange("p (t n) -> p t n", t=NT)
        kcvcT = kT[:, 0:2, :]
        lat = kfull[:, :, :, :].rearrange("p t h n -> p (t h n)")[:, 0:768]
        cqn = lat[:, 0:512].rearrange("p (t n) -> p t n", t=NT)
        ckvn = lat[:, 512:768].rearrange("p (t n) -> p t n", t=NT)
        vbd = proj[:, 0, 0:512].rearrange("p (h d) -> p h d", h=8)
        hx, hy, hz = (proj[0:64, 1, i * 128:(i + 1) * 128] for i in range(3))
        hk = proj[:, 1, 384:448]
        kc = proj[0:32, 1, 448:512]
        kcr = proj[0:32, 1, 512:576]
        kcmpT = proj[0:64, 1, 576:608]
        vrep = proj[:, 1, 608:672]
        mq = xT
        mixT = mix[:, :, :].rearrange("p t n -> p (t n)").rearrange("p (k t) -> p k t", k=KD)
        cqT = mixT[:, 0:2, :]
        ckvT = mixT[:, 2, :]
        mflat = mix[:, :, :].rearrange("p t n -> p (t n)")
        selT = mflat[:, 0:256].bitcast(BF16).rearrange("p (b t) -> p b t", b=2)
        yb = xT[:, 0:6, :].rearrange("p k t -> p (k t)").bitcast(BF16).rearrange("p (a d) -> p a d", a=3)
        y_rest = tmp
        selb = mflat[:, 1024:1152].bitcast(BF16).rearrange("p (t c) -> p t c", t=NT)
        selg = mflat[:, 1152:1408].rearrange("p (t c) -> p t c", t=NT)
        sil = mflat[:, 1408:1664]
        h_sb = mflat[:, 1664:1920]
        xg = p_sb[:, :, :].rearrange("p a n -> p (a n)").rearrange("p (k c) -> p k c", k=KD)
        comb = pt_sb
        sil_sh = tmp[:, 0, :]
        h_sh = tmp[:, 1, :].rearrange("p (j t) -> p j t", j=2)
        xb = mring[:, 2, 1024:4096].bitcast(BF16).rearrange("p (a t d) -> p a t d", a=3, t=NT)
        rest = mix
        rout = kfull[:, :, :, :].rearrange("p t h n -> p (t h n)")

        def rt(i):
            return rout[:, i * 128:(i + 1) * 128]
        score, choice, masked, replaced, picked, gate_w, rank = (
            rt(i).rearrange("p (t e) -> p t e", t=NT) for i in range(7))
        best8 = rt(7).rearrange("p (g n) -> p g n", n=8)
        cmpA, cmpB = rt(8), rt(9)
        grp = rt(10)[:, 0:16]
        gmask = rt(10)[:, 16:32]
        pen = rt(10)[:, 32:48]
        top8 = rt(10)[:, 48:64]
        wsum = rt(10)[:, 64:68]
        ident = cst[:, CONST["ident"][0]:CONST["ident"][0] + P]

        def con(name):
            a, w = CONST[name]
            return cst[:, a:a + w]
        rope64 = con("rope64").rearrange("p (t s n) -> p t s n", t=NT, s=2)
        rope32 = con("rope32").rearrange("p (t s n) -> p t s n", t=NT, s=2)
        ropec = con("ropec")[0:32, :].rearrange("p (s n) -> p s n", s=2)

        def wg(s):
            return ring[:, s, 0:KD * FF].rearrange("p (k f) -> p k f", k=KD)

        def wu(s):
            return ring[:, s, KD * FF:2 * KD * FF].rearrange("p (k f) -> p k f", k=KD)

        def wgu(s):
            return ring[:, s, 0:2 * KD * FF].rearrange("p (m k f) -> p m k f", m=2, k=KD)

        def wd(s):
            return ring[:, s, 2 * KD * FF:SLOT].rearrange("p (j d) -> p j d", j=FF // P)

        x_in = sem("x_in")
        table_in = sem("table_in")
        masks_in = sem("masks_in")
        masks_cast = sem("masks_cast")
        chunk_in = [sem(f"chunk_in{i}") for i in range(MR)]
        ln_in = sem("ln_in")
        ln_used = sem("ln_used")
        work_full = [sem(f"work_full{i}") for i in range(2)]
        work_free = [sem(f"work_free{i}") for i in range(2)]
        x_ready = sem("x_ready")
        roped = sem("roped")
        s_scores = sem("s_scores")
        s_max = sem("s_max")
        s_scaled = sem("s_scaled")
        s_exp = sem("s_exp")
        s_pt = sem("s_pt")
        s_ptcopy = sem("s_ptcopy")
        s_pv = sem("s_pv")
        o_taken = [sem(f"o_taken{i}") for i in range(NT)]
        act_gate = sem("act_gate")
        act_std = sem("act_std")
        var_ready = sem("var_ready")
        act_hid = sem("act_hid")
        hid_in = sem("hid_in")
        sig_ready = sem("sig_ready")
        routed = sem("routed")
        picked_ready = sem("picked_ready")
        dve_chain = sem("dve_chain")
        sh_gu = sem("sh_gu")
        sh_silu = sem("sh_silu")
        sh_h = sem("sh_h")
        part_ready = sem("part_ready")
        rest_ready = sem("rest_ready")
        experts_done = sem("experts_done")
        out_done = sem("out_done")
        L = [dict((n, sem(f"{n}_{l}")) for n in (
            "gu_in0", "gu_in1", "gu_in2", "gu_in3", "dn_in0", "dn_in1", "dn_in2", "dn_in3", "sel_ready", "xg_full", "xg_copied", "sel0_full", "sel0_copied",
            "ht_full", "ht_copied", "gu_full", "silu_done", "h_ready", "y_full", "y_part", "y_left", "y_split", "selT_ready", "window_done", "sel_chain",
            "rank_moved"))
             for l in range(2)]

        def value(stage):
            n = WORK[stage]
            return n % 2, n // 2

        block = ctx.enter_context(nc.Block())
        p_names = ("l0_", "l1_")

        ROPED = {}
        for i, n in enumerate(("q", "ks", "blocks", "kw", "kv_lat", "hk", "cmpk", "vbd", "mlaq", "mlak", "q0", "k0", "q1", "k1")):
            ROPED[n] = i + 1

        @block.sync
        def _(sp):
            sp.dma_start(x[:, :, :], A["x"][0].rearrange("(t p) d -> p t d", p=P)).then_inc(x_in, 16)
            sp.dma_start(cst[:, :], table).then_inc(table_in, 16)
            sp.dma_start(scratch[:, 0:N_MASK], masks).then_inc(masks_in, 16)
            sp.dma_start(pe_sb[:, :], peT).then_inc(masks_in, 16)
            for l in range(2):
                S, pre = L[l], p_names[l]

                def weights(name, e):
                    if isinstance(e, int):
                        return A[f"{pre}exp_{name}"][e]
                    return A[f"{pre}exp_{name}"][bass.ds(e, 1)].rearrange("a k f -> (a k) f")

                def load_gate_up(s, g_src, u_src):
                    sp.dma_start(wg(s), g_src.rearrange("(p k) f -> p k f", k=KD)).then_inc(S[f"gu_in{s}"], 16)
                    sp.dma_start(wu(s), u_src.rearrange("(p k) f -> p k f", k=KD)).then_inc(S[f"gu_in{s}"], 16)

                def load_down(s, d_src):
                    sp.dma_start(wd(s), d_src.rearrange("(j p) d -> p j d", p=P)).then_inc(S[f"dn_in{s}"], 16)

                def expert_gate_up(s, e):
                    load_gate_up(s, weights("gate", e), weights("up", e))

                def expert_down(s, e):
                    load_down(s, weights("down", e))

                if l == 0:
                    sp.wait_ge(chunk_in[2], 16)
                else:
                    sp.wait_ge(experts_done, 1)
                load_gate_up(0, A[pre + "sh_gate"], A[pre + "sh_up"])
                load_down(0, A[pre + "sh_down"])
                expert_gate_up(1, 0)
                expert_down(1, 0)
                for t in range(NT):
                    sp.wait_ge(o_taken[t], 2 * l + 2)
                for e in (1, 2):
                    expert_gate_up(e + 1, e)
                    expert_down(e + 1, e)
                sp.wait_ge(sh_gu, l + 1)
                expert_gate_up(0, 3)
                sp.wait_ge(routed, l + 1)
                windows = sp.value_load(nwin_i[0:1, 0:1], min_val=1, max_val=4)

                def pair_gate_up(w, i, q):
                    sp.wait_ge(S["gu_full"], w * PAIRS + i * 2 + (q - 1))
                    for b, s in enumerate(((1, 2), (3, 0))[q % 2]):
                        expert_gate_up(s, i * 4 + (2 * q + b))

                def pair_down(w, i, q):
                    sp.wait_ge(S["y_full"], w * (2 * PAIRS) + i * 4 + 2 * q)
                    for b, s in enumerate(((1, 2), (3, 0))[q % 2]):
                        expert_down(s, i * 4 + (2 * q + b))
                pair_gate_up(0, 0, 2)
                sp.wait_ge(S["y_full"], 2)
                expert_down(0, 3)
                with sp.Fori(0, windows) as w:
                    with sp.Fori(0, 14) as i:
                        for q in (2, 3):
                            pair_down(w, i, q)
                            pair_gate_up(w, i, q + 1)
                    pair_down(w, 14, 2)
                    pair_gate_up(w, 14, 3)
                    pair_down(w, 14, 3)
                    with sp.If(w + 1 < windows):
                        for e in range(4):
                            sp.wait_ge(S["y_full"], w * (2 * PAIRS) + 2 * (PAIRS if e < 2 else PAIRS + 1))
                            expert_gate_up((e + 1) % RING, e)
                            expert_down((e + 1) % RING, e)
                        pair_gate_up(w + 1, 0, 2)
            for t in range(NT):
                sp.wait_ge(x_ready, 3 * NT + t + 1)
                sp.dma_start(out[0, t * P:(t + 1) * P, :], x[:, t, :]).then_inc(out_done, 16)
            sp.wait_ge(out_done, 16 * NT)

        @block.gpsimd
        def _(pool):
            c = 0

            def next_chunk():
                nonlocal c
                if c >= MR:
                    b, v = value(LAST_USE[c - MR])
                    pool.wait_ge(work_full[b], v + 1)
                c += 1
                return (c - 1) % MR

            def columns(src, a, w, rows="(p k) n -> p k n"):
                s = next_chunk()
                pool.dma_start(mring[:, s, 0:KD * w].rearrange("p (k n) -> p k n", k=KD),
                               src[:, a:a + w].rearrange(rows, k=KD)).then_inc(chunk_in[s], 16)

            def norm_params(l, which, n):
                if n:
                    pool.wait_ge(ln_used, n)
                for i, k in enumerate("gb"):
                    pool.dma_start(lnp[:, i, :], A[f"l{l}_ln{which}_{k}"].partition_broadcast(P)).then_inc(ln_in, 16)

            for l in range(2):
                pre = p_names[l]
                if l == 0:
                    for a, w in IN_CHUNKS:
                        columns(A[pre + "w_in"], a, w)
                    norm_params(0, 1, 0)
                    s = next_chunk()
                    for i, k in enumerate(("cmp_k1", "cmp_v1")):
                        pool.dma_start(mring[64 * i:64 * i + 64, s, :].rearrange("p (l n) -> p l n", n=P),
                                       A[pre + "nsa_" + k].rearrange("(l d) n -> d l n", d=HD)).then_inc(chunk_in[s], 16)
                    s = next_chunk()
                    m = mring[:, s, :]
                    pool.dma_start(m[:, 0:1536].rearrange("p (k n) -> p k n", k=2),
                                   A[pre + "mla_w_uq"].rearrange("(p k) n -> p k n", k=2)).then_inc(chunk_in[s], 16)
                    pool.dma_start(m[:, 1536:2560], A[pre + "mla_w_ukv"]).then_inc(chunk_in[s], 16)
                    pool.dma_start(m[:, 2560:2624], A[pre + "nsa_cmp_k2"]).then_inc(chunk_in[s], 16)
                    pool.dma_start(m[:, 2624:2688], A[pre + "nsa_cmp_v2"]).then_inc(chunk_in[s], 16)
                    pool.dma_start(m[:, 2688:2944], A[pre + "mla_q_norm"].partition_broadcast(P)).then_inc(chunk_in[s], 16)
                    pool.dma_start(m[:, 2944:3072], A[pre + "mla_kv_norm"].partition_broadcast(P)).then_inc(chunk_in[s], 16)
                else:
                    for n in range(6):
                        if n == 2:
                            pool.wait_ge(experts_done, 1)
                        columns(A[pre + "w_qkv"], (n % 3) * D + (n // 3) * 512, 512)
                    norm_params(1, 1, 2)
                for n in range(2):
                    columns(A[pre + "w_out"], n * 512, 512, "(k p) n -> p k n")
                s = next_chunk()
                pool.dma_start(mring[:, s, 0:512].rearrange("p (k n) -> p k n", k=KD),
                               A[pre + "router"].rearrange("(p k) n -> p k n", k=KD)).then_inc(chunk_in[s], 16)
                pool.dma_start(mring[:, s, 512:576], A[pre + "router_bias"].partition_broadcast(P)).then_inc(chunk_in[s], 16)
                norm_params(l, 2, 2 * l + 1)

        CHUNKS = [16] * 4 + [32, 96, 16, 16, 32] + [16] * 8 + [32]
        chunk_value = [sum(CHUNKS[i] for i in range(n % MR, n + 1, MR)) for n in range(len(CHUNKS))]

        def chunk_landed(eng, n):
            eng.wait_ge(chunk_in[n % MR], chunk_value[n])
            return mring[:, n % MR, :]

        @block.tensor
        def _(pe):
            mm = pe.matmul

            def open_work(stage):
                b, v = value(stage)
                if v:
                    pe.wait_ge(work_free[b], v)
                return work[b]

            def close_work(ins, stage):
                ins.then_inc(work_full[value(stage)[0]], 1)

            def copied(stage):
                b, v = value(stage)
                pe.wait_ge(work_free[b], v + 1)

            def transposed(l, name, src, tiles):
                for t in range(NT):
                    if tiles:
                        pe.wait_ge(x_ready, tiles - NT + t + 1)
                    for kh in range(2):
                        w = open_work((l, name, t, kh))
                        for i in range(4):
                            ins = pe.transpose(w[:, i * P:(i + 1) * P], src[:, t, 4 * kh + i::KD], ident)
                        close_work(ins, (l, name, t, kh))

            def head_transposes(stages, src, width):
                for t in range(NT):
                    for half in range(2):
                        w = open_work(stages + (t, half))
                        for i in range(4):
                            ins = pe.transpose(w[0:width, i * P:(i + 1) * P], src(t, 4 * half + i), ident)
                        close_work(ins, stages + (t, half))

            def product(l, name, n, src, chunk, width, tiles=range(NT)):
                m = chunk_landed(pe, chunk)[:, 0:KD * width].rearrange("p (k n) -> p k n", k=KD)
                for t in tiles:
                    w = open_work((l, name, n, t))
                    for k in range(KD):
                        ins = mm(w[:, 0:width], src[:, k, t * P:(t + 1) * P], m[:, k, :],
                                 start=(k == 0), stop=(k == KD - 1))
                    close_work(ins, (l, name, n, t))

            def scores(u, mask, parts):
                s = s_bank[u % 2]
                if u >= 2:
                    pe.wait_ge(s_exp, u - 1)
                mm(s[:, 0:parts[-1][1]], identb[:, :], mask, start=True, stop=False, skip_group_check=True)
                for a, b, q, k in parts:
                    ins = mm(s[:, a:b], q, k, start=False, stop=(b == parts[-1][1]), skip_group_check=True)
                ins.then_inc(s_scores, 1)

            def unit_scores(u, qt, heads, q, k):
                nk = (qt + 1) * P
                mask = maskb[:, 128 - 128 * qt:256] if qt else maskb[:, 128:256]
                reps = len(heads)
                scores(u, mask.unsqueeze(1).broadcast_to([P, reps, nk]),
                       [(i * nk, (i + 1) * nk, q(h, qt), k(h, nk)) for i, h in enumerate(heads)])

            def unit_transposes(u, n):
                pe.wait_ge(s_scaled, u + 1)
                if u >= 2:
                    pe.wait_ge(s_ptcopy, u - 1)
                for i in range(n):
                    ins = pe.transpose(pt_bank[u % 2][:, i * P:(i + 1) * P], p_of(u)[:, i * P:(i + 1) * P], ident)
                ins.then_inc(s_pt, 1)

            def open_sums(sums):
                for t in range(NT):
                    if sums:
                        pe.wait_ge(o_taken[t], sums)
                    mm(o_bank[t][:, :], maskb[:, 0:P], maskb[:, 0:512], start=True, stop=False, skip_group_check=True)

            def unit_values(u, qt, heads, v):
                pe.wait_ge(s_ptcopy, u + 1)
                for kb in range(qt + 1):
                    for i, h in enumerate(heads):
                        b = (h % 2) * HD
                        ins = mm(o_bank[qt][b:b + HD, h // 2 * P:(h // 2 + 1) * P], v(h, kb),
                                 pt_sb[:, u % 2, (i * (qt + 1) + kb) * P:(i * (qt + 1) + kb + 1) * P],
                                 start=False, stop=False, skip_group_check=True)
                ins.then_inc(s_pv, 1)

            def attention(l, operands, between):
                units = CHAINS[l]
                for n in range(len(units) + 3):
                    if n < len(units):
                        g, i = units[n]
                        u = UNITS[g] + i
                        if g == "cmp":
                            scores(u, maskb[:, 256 + i * P:256 + (i + 1) * P],
                                   [(h * NC, (h + 1) * NC, q_nsa(h, i), kcmpT[:, (h // R) * NC:(h // R + 1) * NC])
                                    for h in range(8)])
                        else:
                            unit_scores(u, *GROUP[i], *operands[g][0:2])
                    if 0 <= n - 2 < len(units):
                        g, i = units[n - 2]
                        unit_transposes(UNITS[g] + i, 1 if g == "cmp" else 4)
                    if n >= 3:
                        g, i = units[n - 3]
                        u = UNITS[g] + i
                        if i == 0 and g in OPENS:
                            open_sums({"sel": 0, "mla": 1, "h0": 2, "h1": 3}[g])
                        if g == "cmp":
                            pe.wait_ge(s_ptcopy, u + 1)
                            if i == 0:
                                pe.wait_ge(roped, ROPED["vbd"])
                            for c in range(4):
                                ins = mm(o_bank[i][:, c * P:(c + 1) * P], vbd[:, 2 * c:2 * c + 2, :].rearrange("p h d -> p (h d)"),
                                         pt_sb[:, u % 2, 0:P], start=False, stop=False, skip_group_check=True)
                            ins.then_inc(s_pv, 1)
                        else:
                            unit_values(u, *GROUP[i], operands[g][2])
                    if n in between:
                        between[n]()

            def q_nsa(h, qt):
                return qT[0:HD, h, qt * P:(qt + 1) * P]

            pe.wait_ge(x_in, 16)
            pe.wait_ge(table_in, 16)
            for l in range(2):
                S = L[l]
                transposed(l, "xT", x, 2 * l * NT)

                def turned(name, t):
                    for kh in range(2):
                        copied((l, name, t, kh))
                if l == 0:
                    for t in range(NT):
                        turned("xT", t)
                        product(0, "proj", 0, xT, 0, 512, [t])
                    product(0, "proj", 1, xT, 1, 512)
                    pe.wait_ge(roped, ROPED["q"])
                    head_transposes((0, "qT"), lambda t, h: qr[:, t, h * HD:(h + 1) * HD], HD)
                    w = open_work((0, "kcvc"))
                    copied((0, "proj", 1, 0))
                    copied((0, "proj", 1, 1))
                    for g in range(G):
                        for t in range(NT):
                            ins = pe.transpose(w[:, g * T + t * P:g * T + (t + 1) * P], proj[:, t, C_KC + g * P:C_KC + (g + 1) * P], ident)
                    close_work(ins, (0, "kcvc"))

                    def turn_keys(kind, stage):
                        pe.wait_ge(roped, ROPED[stage])
                        w = open_work((0, "kT", kind))
                        for g in range(G):
                            for t in range(NT):
                                a = kind * P + g * HD
                                ins = pe.transpose(w[0:HD, g * T + t * P:g * T + (t + 1) * P], kr0[:, t, a:a + HD], ident)
                        close_work(ins, (0, "kT", kind))
                    product(0, "proj", 2, xT, 2, 512)
                    turn_keys(0, "ks")
                    product(0, "proj", 3, xT, 3, IN_CHUNKS[3][1])
                    turn_keys(1, "kw")
                    m = chunk_landed(pe, 4)
                    pe.wait_ge(roped, ROPED["blocks"])
                    w = open_work((0, "hid"))
                    for i in range(CMP_LEN):
                        ins = mm(w[0:64, 0:P], blocks[:, i].rearrange("p a g c -> p (a g c)"), m[:, i * P:(i + 1) * P],
                                 start=(i == 0), stop=(i == CMP_LEN - 1))
                    close_work(ins, (0, "hid"))
                    for t in range(NT):
                        for h in range(2):
                            copied((0, "qT", t, h))
                    copied((0, "kT", 0))
                    copied((0, "kT", 1))
                    copied((0, "proj", 2, 1))
                    pe.wait_ge(masks_cast, 1)
                    m5 = mring[:, 5 % MR, :]

                    def turn_latents():
                        pe.wait_ge(roped, ROPED["kv_lat"])
                        w = open_work((0, "cq"))
                        for k in range(2):
                            for t in range(NT):
                                ins = pe.transpose(w[:, k * T + t * P:k * T + (t + 1) * P], cqn[:, t, k::2], ident)
                        close_work(ins, (0, "cq"))
                        w = open_work((0, "ckv"))
                        for t in range(NT):
                            ins = pe.transpose(w[:, t * P:(t + 1) * P], ckvn[:, t, :], ident)
                        close_work(ins, (0, "ckv"))

                    def turn_hidden():
                        pe.wait_ge(roped, ROPED["hk"])
                        w = open_work((0, "hkT"))
                        close_work(pe.transpose(w[:, 0:64], hx, ident[0:64, 0:64]), (0, "hkT"))

                    def compressed():
                        chunk_landed(pe, 5)
                        w = open_work((0, "kcmp"))
                        pe.wait_ge(hid_in, 1)
                        mm(w[0:32, 0:64], hk[:, 0:32], m5[:, 2560:2624], start=True, stop=True)
                        ins = mm(w[:, 64:128], tmp[:, 0, 0:128], m5[:, 2624:2688], start=True, stop=True)
                        close_work(ins, (0, "kcmp"))

                    def compressed_keys():
                        w = open_work((0, "kcmpT"))
                        pe.wait_ge(roped, ROPED["cmpk"])
                        close_work(pe.transpose(w[0:64, 0:32], kcr, ident[0:32, 0:32]), (0, "kcmpT"))

                    def mla_queries(t):
                        copied((0, "cq"))
                        for half in range(2):
                            w = open_work((0, "uq", t, half))
                            for k in range(2):
                                ins = mm(w[:, 0:384], cqT[:, k, t * P:(t + 1) * P],
                                         m5[:, k * 768 + half * 384:k * 768 + (half + 1) * 384],
                                         start=(k == 0), stop=(k == 1))
                            close_work(ins, (0, "uq", t, half))

                    def mla_keys(t):
                        copied((0, "ckv"))
                        for half in range(2):
                            w = open_work((0, "ukv", t, half))
                            ins = mm(w[:, :], ckvT[:, t * P:(t + 1) * P],
                                     m5[:, 1536 + half * 512:1536 + (half + 1) * 512], start=True, stop=True)
                            close_work(ins, (0, "ukv", t, half))

                    def turn_mla_keys():
                        pe.wait_ge(roped, ROPED["mlak"])
                        head_transposes((0, "mkT"), lambda t, h: kfull[:, t, h, :], QK)

                    def turn_mla_queries():
                        head_transposes((0, "mqT"), lambda t, h: mlaq[:, t, h, :], QK)

                    def before_compressed():
                        copied((0, "kcmpT"))

                    def before_mla():
                        for t in range(NT):
                            for h in range(2):
                                copied((0, "mkT", t, h))
                                copied((0, "mqT", t, h))
                    attention(0, {
                        "sel": (q_nsa, lambda h, nk: kTn[:, 0, h // R, 0:nk],
                                lambda h, kb: proj[:, kb, C_VS + h // R * HD:C_VS + (h // R + 1) * HD]),
                        "win": (q_nsa, lambda h, nk: kTn[:, 1, h // R, 0:nk],
                                lambda h, kb: proj[:, kb, C_VW + h // R * HD:C_VW + (h // R + 1) * HD]),
                        "mla": (lambda h, qt: mq[0:QK, h, qt * P:(qt + 1) * P], lambda h, nk: kT[0:QK, h, 0:nk],
                                lambda h, kb: ukv[:, kb, h * P + HD:(h + 1) * P])},
                        {1: turn_latents, 2: turn_hidden, 3: compressed, 4: compressed_keys,
                         5: lambda: mla_queries(0), 6: lambda: mla_queries(1), 7: lambda: mla_keys(0),
                         8: lambda: mla_keys(1), 10: turn_mla_keys, 11: before_compressed, 12: turn_mla_queries,
                         13: before_mla})
                    chunk0 = 6
                else:
                    for half in range(2):
                        for t in range(NT):
                            if half == 0:
                                turned("xT", t)
                            product(1, "proj", 3 * half, xT, 9 + 3 * half, 512, [t])
                        product(1, "proj", 3 * half + 1, xT, 10 + 3 * half, 512)
                        product(1, "proj", 3 * half + 2, xT, 11 + 3 * half, 512)
                        pe.wait_ge(roped, ROPED[f"q{half}"])
                        head_transposes((1, "qT", half), lambda t, h: qr1[:, t, h * HD:(h + 1) * HD], HD)
                        pe.wait_ge(roped, ROPED[f"k{half}"])
                        head_transposes((1, "kT", half), lambda t, h: kr1[:, t, h * HD:(h + 1) * HD], HD)
                    for half in range(2):
                        for t in range(NT):
                            copied((1, "proj", 3 * half + 2, t))
                            for h in range(2):
                                copied((1, "qT", half, t, h))
                                copied((1, "kT", half, t, h))
                    attention(1, {f"h{half}": (lambda h, qt, half=half: qTh[half][0:HD, h, qt * P:(qt + 1) * P],
                                               lambda h, nk, half=half: kTh[half][0:HD, h, 0:nk],
                                               lambda h, kb, half=half: vmoba[:, half, kb, h * HD:(h + 1) * HD])
                                  for half in range(2)}, {})
                    chunk0 = 15
                for t in range(NT):
                    pe.wait_ge(o_taken[t], 2 * l + 2)
                    for n in range(2):
                        product(l, "out", n, mixT, chunk0 + n, 512, [t])
                transposed(l, "yT", x, (2 * l + 1) * NT)
                m = chunk_landed(pe, chunk0 + 2)[:, 0:512].rearrange("p (k n) -> p k n", k=KD)
                w = open_work((l, "router"))
                for t in range(NT):
                    turned("yT", t)
                    for k in range(KD):
                        ins = mm(w[:, t * E_N:(t + 1) * E_N], xT[:, k, t * P:(t + 1) * P], m[:, k, :],
                                 start=(k == 0), stop=(k == KD - 1))
                close_work(ins, (l, "router"))
                pe.wait_ge(S["gu_in0"], 32)
                for b, mat in enumerate((wg(0), wu(0))):
                    for j in range(2):
                        if b == j == 1:
                            w = open_work((l, "rank"))
                            pe.wait_ge(picked_ready, l + 1)
                            before, ones = con("before"), con("ones")
                            mm(w[:, 0:64], before, picked[:, 0, :], start=True, stop=True)
                            mm(w[:, 64:128], ones, picked[:, 0, :], start=True, stop=False)
                            mm(w[:, 64:128], before, picked[:, 1, :], start=False, stop=True)
                            mm(w[:, 128:192], ones, picked[:, 0, :], start=True, stop=False)
                            close_work(mm(w[:, 128:192], ones, picked[:, 1, :], start=False, stop=True), (l, "rank"))
                        for k in range(KD):
                            ins = mm(s_bank[b][:, j * T:(j + 1) * T], mat[:, k, j * P:(j + 1) * P], xT[:, k, :],
                                     start=(k == 0), stop=(k == KD - 1))
                ins.then_inc(sh_gu, 1)
                pe.wait_ge(routed, l + 1)
                copied((l, "rank"))
                pe.wait_ge(part_ready, 6 * (l + 1))
                windows = pe.value_load(nwin_i[0:1, 0:1], min_val=1, max_val=4)

                def gather(at, half):
                    if half == 0:
                        pe.wait_ge(S["sel_ready"], at + 1)
                    else:
                        pe.wait_ge(S["xg_copied"], at * 2 + 1)
                    for i in range(4):
                        n = 0
                        for t in range(NT):
                            for part in range(3):
                                ins = mm(bank[0][:, i * P:(i + 1) * P], xb[:, part, t, 4 * half + i::KD], selb[:, t, :],
                                         start=(n == 0), stop=(n == 5))
                                n += 1
                    ins.then_inc(S["xg_full"], 1)

                def turn_sel():
                    for t in range(NT):
                        ins = pe.transpose(bank[1][:, T + t * P:T + (t + 1) * P], selg[:, t, :], ident)
                    return ins

                def turn_h(at):
                    pe.wait_ge(S["h_ready"], at + 1)
                    for j in range(2):
                        ins = pe.transpose(bank[1][:, j * P:(j + 1) * P], h_sb[:, j * P:(j + 1) * P], ident)
                    return ins

                def gate_up(at, slots):
                    pe.wait_ge(S["xg_copied"], at * 2 + 2)
                    for s, v in slots:
                        pe.wait_ge(S[f"gu_in{s}"], v * 32)
                    for k in range(KD):
                        for b, (s, _) in enumerate(slots):
                            ins = mm(bank[1][b * CAP:(b + 1) * CAP, :], xg[:, k, b * CAP:(b + 1) * CAP], wgu(s)[:, :, k, :],
                                     start=(k == 0), stop=(k == KD - 1))
                    ins.then_inc(S["gu_full"], 1)

                def down(at, slots, buf):
                    pe.wait_ge(S["ht_copied"], at + 1)
                    for s, v in slots:
                        pe.wait_ge(S[f"dn_in{s}"], v * 16)
                    for n in range(2):
                        for j in range(2):
                            for b, (s, _) in enumerate(slots):
                                ins = mm(s_bank[n][b * CAP:(b + 1) * CAP, :], comb[:, buf, j * P + b * CAP:j * P + (b + 1) * CAP],
                                         wd(s)[:, j, n * 512:(n + 1) * 512], start=(j == 0), stop=(j == 1))
                        ins.then_inc(S["y_full"], 1)

                def scatter(at, buf):
                    pe.wait_ge(S["selT_ready"], at + 1)
                    for n in range(2):
                        pe.wait_ge(S["y_split"], at * 2 + (n + 1))
                        for t in range(NT):
                            for part in range(3):
                                ins = mm(bank[4 + 2 * t + n][:, :], selT[:, buf, t * P:(t + 1) * P],
                                         yb[:, part, n * 512:(n + 1) * 512], start=False, stop=False, skip_group_check=True)
                    return ins

                def start(w):
                    gather(w * PAIRS, 0)
                    turn_sel().then_inc(S["sel0_full"], 1)
                    gather(w * PAIRS, 1)
                    pe.wait_ge(S["sel0_copied"], w + 1)
                    v = w * (E_N // RING)
                    gate_up(w * PAIRS, ((1, v + 1), (2, v + 1)))

                def pair(w, i, j, first=False, last=False):
                    at = w * PAIRS + i * 2 + j
                    v = w * (E_N // RING) + i
                    slots = ((3, v + 1), (0, v + 2)) if j else ((1, v + 1), (2, v + 1))
                    if not first:
                        gate_up(at, slots)
                    if not last:
                        gather(at + 1, 0)
                    if not first:
                        scatter(at - 1, 1 - j)
                    ins = turn_h(at)
                    if not last:
                        ins = turn_sel()
                    ins.then_inc(S["ht_full"], 1)
                    if not last:
                        gather(at + 1, 1)
                    down(at, slots, j)

                start(0)
                pe.wait_ge(sh_h, l + 1)
                pe.wait_ge(S["dn_in0"], 16)
                for j in range(2):
                    for t in range(NT):
                        for n in range(2):
                            ins = mm(bank[4 + 2 * t + n][:, :], h_sh[:, j, t * P:(t + 1) * P],
                                     wd(0)[:, j, n * 512:(n + 1) * 512], start=(j == 0), stop=False,
                                     skip_group_check=True)
                            if j == t == 1:
                                ins.then_inc(S["y_full"], 1)
                for t in range(NT):
                    for n in range(2):
                        mm(bank[4 + 2 * t + n][:, :], con("alpha"), x[:, t, n * 512:(n + 1) * 512],
                           start=False, stop=False, skip_group_check=True)
                with pe.Fori(0, windows) as w:
                    for j in range(2):
                        pair(w, 0, j, first=(j == 0))
                    with pe.Fori(1, 15) as i:
                        for j in range(2):
                            pair(w, i, j)
                    for j in range(2):
                        pair(w, 15, j, last=(j == 1))
                    scatter(w * PAIRS + (PAIRS - 1), 1).then_inc(S["window_done"], 1)
                    with pe.If(w + 1 < windows):
                        start(w + 1)

        @block.scalar
        def _(act):
            cp = ACT.Copy

            def full(stage):
                b, v = value(stage)
                act.wait_ge(work_full[b], v + 1)
                return work[b]

            def free(ins, stage):
                ins.then_inc(work_free[value(stage)[0]], 1)

            def take(stage, dst, src=lambda w: w[:, :], scale=1.0):
                free(act.activation(dst, src(full(stage)), cp, scale=scale), stage)

            def unit_exp(g, i):
                u = UNITS[g] + i
                act.wait_ge(s_max, u + 1)
                if u >= NP:
                    act.wait_ge(s_pt, u - NP + 1)
                p = p_of(u)
                if g == "cmp":
                    ins = act.activation(p[:, 0:P], p[:, 0:P], ACT.Exp)
                else:
                    qt, heads = GROUP[i]
                    nk = (qt + 1) * P
                    for a, h in enumerate(heads):
                        ins = act.activation(p[:, a * nk:(a + 1) * nk], s_bank[u % 2][:, a * nk:(a + 1) * nk],
                                             ACT.Exp, bias=negmax[:, u % 2, a:a + 1],
                                             accum_out=rsum[:, qt, h:h + 1])
                ins.then_inc(s_exp, 1)

            def unit_turn(g, i):
                u = UNITS[g] + i
                w = P if g == "cmp" else 512
                act.wait_ge(s_pt, u + 1)
                if u >= 2:
                    act.wait_ge(s_pv, u - 1)
                act.activation(pt_sb[:, u % 2, 0:w], pt_bank[u % 2][:, 0:w], cp).then_inc(s_ptcopy, 1)

            def attention(l, between):
                units = CHAINS[l]
                for n in range(len(units) + 3):
                    if n < len(units):
                        unit_exp(*units[n])
                    if 0 <= n - 2 < len(units):
                        unit_turn(*units[n - 2])
                    if n >= 3:
                        g, i = units[n - 3]
                        if g in SUMS and (n - 2 == len(units) or units[n - 2][0] != g):
                            act.wait_ge(s_pv, UNITS[g] + i + 1)
                            act.activation(mixT[:, SUMS[g]:SUMS[g] + 4, 0:P],
                                           o_bank[0][:, :].rearrange("p (k q) -> p k q", k=4), cp).then_inc(o_taken[0], 1)
                    for f in between.get(n, ()):
                        f()

            def roots(n, count):
                act.wait_ge(var_ready, n)
                act.activation(std[:, 0:count], var[:, 0:count], ACT.Sqrt).then_inc(act_std, 1)

            n_var = 0
            for l in range(2):
                S = L[l]
                for kh in range(2):
                    take((l, "xT", 0, kh), xT[:, 4 * kh:4 * kh + 4, 0:P], lambda w: w[:, :].rearrange("p (k n) -> p k n", k=4))
                if l == 0:
                    act.wait_ge(masks_cast, 1)
                    take((0, "proj", 0, 0), proj[:, 0, 0:512])
                    act.activation(kv_pairs(0), full((0, "proj", 1, 0))[:, 0:256].rearrange("p (a g d) -> p a g d", a=2, g=G), cp)
                    take((0, "proj", 1, 0), proj[:, 0, C_KS:C_KW], lambda b: b[:, 256:512])
                    for h in range(2):
                        take((0, "qT", 0, h), qT[0:64, 4 * h:4 * h + 4, 0:P],
                             lambda w: w[0:64, :].rearrange("p (h n) -> p h n", h=4), scale=HD ** -0.5)
                    take((0, "proj", 2, 0), proj[:, 0, 1024:1536])
                    take((0, "kT", 0), kTn[:, 0, :, :], lambda w: w[0:64, :].rearrange("p (g n) -> p g n", g=G))
                    take((0, "proj", 3, 0), proj[:, 0, 1536:W_IN], lambda b: b[:, 0:W_IN - 1536])
                    take((0, "kT", 1), kTn[:, 1, :, :], lambda w: w[0:64, :].rearrange("p (g n) -> p g n", g=G))
                    n_var += 1
                    roots(n_var, 4)
                    for b in range(2):
                        bb, v = value((0, "proj", 2, b))
                        act.wait_ge(work_free[bb], v + 1)
                    act.activation(gates[:, :, :], proj[:, :, C_GATE:C_GATE + 24], ACT.Exp, scale=-1.0).then_inc(act_gate, 1)

                    def hidden_exp():
                        act.wait_ge(act_hid, 1)
                        act.activation(hz, hy, ACT.Exp, scale=-2.0 * (2.0 / np.pi) ** 0.5).then_inc(act_gate, 1)

                    def latents():
                        take((0, "cq"), cqT, lambda w: w[:, :].rearrange("p (k n) -> p k n", k=2))
                        take((0, "ckv"), ckvT, lambda w: w[:, 0:T])

                    def mla_queries():
                        for half in range(2):
                            take((0, "uq", 0, half), mlaq[:, 0, 4 * half:4 * half + 4, :],
                                 lambda w: w[:, 0:384].rearrange("p (h n) -> p h n", h=4), scale=QK ** -0.5)

                    def mla_keys():
                        for half in range(2):
                            take((0, "ukv", 0, half), ukv[:, 0, half * 512:(half + 1) * 512])

                    def turned(name, dst):
                        def run():
                            for h in range(2):
                                take((0, name, 0, h), dst[0:QK, 4 * h:4 * h + 4, 0:P],
                                     lambda w: w[0:QK, :].rearrange("p (h n) -> p h n", h=4))
                        return run
                    attention(0, {0: (hidden_exp,), 1: (latents,), 5: (mla_queries,), 7: (mla_keys,),
                                  10: (turned("mkT", kT),), 12: (turned("mqT", mq),)})
                else:
                    for half in range(2):
                        take((1, "proj", 3 * half + 2, 0), vmoba[:, half, 0, :])
                        for h in range(2):
                            take((1, "qT", half, 0, h), qTh[half][0:HD, 4 * h:4 * h + 4, 0:P],
                                 lambda w: w[0:HD, :].rearrange("p (h n) -> p h n", h=4), scale=HD ** -0.5)
                        for h in range(2):
                            take((1, "kT", half, 0, h), kTh[half][0:HD, 4 * h:4 * h + 4, 0:P],
                                 lambda w: w[0:HD, :].rearrange("p (h n) -> p h n", h=4))
                    attention(1, {})
                def part_of_x(part, t):
                    if part:
                        act.wait_ge(rest_ready, 4 * l + (part - 1) * NT + t + 1)
                    else:
                        act.wait_ge(x_ready, 2 * l * NT + t + 1)
                    act.activation(xb[:, part, t, :], (x, rest, rest)[part][:, t, :], cp).then_inc(part_ready, 1)
                n_var += 1
                roots(n_var, 1)
                chunk_landed(act, 8 + 9 * l)
                part_of_x(0, 0)
                for kh in range(2):
                    take((l, "yT", 0, kh), xT[:, 4 * kh:4 * kh + 4, 0:P],
                         lambda w: w[:, :].rearrange("p (k n) -> p k n", k=4))
                n_var += 1
                roots(n_var, 1)
                part_of_x(0, 1)
                for part in (1, 2):
                    for t in range(NT):
                        part_of_x(part, t)
                w = full((l, "router"))
                act.activation(score, w[:, 0:128].rearrange("p (t e) -> p t e", t=NT), ACT.Exp, scale=-1.0).then_inc(sig_ready, 1)
                act.wait_ge(sh_gu, l + 1)
                act.activation(sil_sh, s_bank[0][:, :], ACT.Silu).then_inc(sh_silu, 1)
                act.wait_ge(routed, l + 1)
                windows = act.value_load(nwin_i[0:1, 0:1], min_val=1, max_val=4)

                def take_xg(at):
                    act.wait_ge(S["xg_full"], at * 2 + 1)
                    act.activation(xg[:, 0:4, :], bank[0][:, :].rearrange("p (k c) -> p k c", k=4), cp).then_inc(S["xg_copied"], 1)

                def silu(at):
                    act.wait_ge(S["gu_full"], at + 1)
                    act.activation(sil, bank[1][:, 0:FF], ACT.Silu).then_inc(S["silu_done"], 1)

                def turned(j, n):
                    a, src = comb[:, j, n * T:(n + 1) * T], bank[1][:, n * T:(n + 1) * T]
                    if n:
                        return act.activation(a, src, cp, accum_out=gate_of[:, 1 - j:2 - j])
                    return act.activation(a, src, cp)

                def split_y(at):
                    for n in range(2):
                        act.wait_ge(S["y_full"], at * 2 + (3 + n))
                        act.activation(yb[:, 0, n * 512:(n + 1) * 512], s_bank[n][:, :], cp).then_inc(S["y_part"], 1)
                    for n in range(2):
                        act.wait_ge(S["y_left"], at * 2 + (n + 1))
                        act.activation(yb[:, 1, n * 512:(n + 1) * 512], y_rest[:, n, :], cp).then_inc(S["y_part"], 1)

                def pair(w, i, j, last=False):
                    at = w * PAIRS + i * 2 + j
                    silu(at)
                    if not last:
                        take_xg(at + 1)
                    act.wait_ge(S["ht_full"], at + 1)
                    if last:
                        turned(j, 0).then_inc(S["ht_copied"], 1)
                    else:
                        turned(j, 1)
                        turned(j, 0).then_inc(S["ht_copied"], 1)
                    split_y(at)

                with act.Fori(0, windows) as w:
                    take_xg(w * PAIRS)
                    act.wait_ge(S["sel0_full"], w + 1)
                    turned(1, 1).then_inc(S["sel0_copied"], 1)
                    with act.Fori(0, 15) as i:
                        for j in range(2):
                            pair(w, i, j)
                    for j in range(2):
                        pair(w, 15, j, last=(j == 1))
                for t in range(NT):
                    n_var += 1
                    roots(n_var, 1)

        @block.vector
        def _(dve):
            chain = 0
            n_std = n_ln = n_split = 0
            tt, ts, stt = dve.tensor_tensor, dve.tensor_scalar, dve.scalar_tensor_tensor

            def link(ins):
                nonlocal chain
                chain += 1
                ins.then_inc(dve_chain, 1)
                dve.wait_ge(dve_chain, chain)

            def full(stage):
                b, v = value(stage)
                dve.wait_ge(work_full[b], v + 1)
                return work[b]

            def copied(stage):
                b, v = value(stage)
                dve.wait_ge(work_free[b], v + 1)

            def free(ins, stage):
                ins.then_inc(work_free[value(stage)[0]], 1)

            def take(stage, dst, src=lambda w: w[:, :], scale=None):
                s = src(full(stage))
                free(dve.tensor_copy(dst, s) if scale is None else ts(dst, s, scale, None, ALU.mult), stage)

            def rope(dst, src, tab, nh, d):
                np_ = src.shape[0]
                h = d // 2
                a = tmp[0:np_, 0, 0:nh * d].rearrange("p (h n) -> p h n", h=nh)
                b = tmp[0:np_, 1, 0:nh * d].rearrange("p (h n) -> p h n", h=nh)

                def bc(v, n):
                    return v.unsqueeze(1).broadcast_to([np_, nh, n])
                tt(a, src, bc(tab[:, 0, :], d), ALU.mult)
                tt(b[:, :, 0:h], src[:, :, h:d], bc(tab[:, 1, 0:h], h), ALU.mult)
                link(tt(b[:, :, h:d], src[:, :, 0:h], bc(tab[:, 1, h:d], h), ALU.mult))
                return tt(dst, a, b, ALU.add)

            def heads(v, nh):
                return v.rearrange("p (h n) -> p h n", h=nh)

            def unit_max(name, n):
                u = UNITS[name] + n
                dve.wait_ge(s_scores, u + 1)
                qt, hs = GROUP[n]
                dve.tensor_reduce(negmax[:, u % 2, 0:len(hs)], heads(s_bank[u % 2][:, :], len(hs)), AX.X, ALU.max,
                                  negate=True).then_inc(s_max, 1)

            def compressed_max(i):
                u = UNITS["cmp"] + i
                dve.wait_ge(s_scores, u + 1)
                dve.wait_ge(s_pt, u - NP + 1)
                s = heads(s_bank[u % 2][:, 0:P], 8)
                link(dve.tensor_reduce(negmax[:, u % 2, 0:8], s, AX.X, ALU.max, negate=True))
                tt(heads(p_of(u)[:, 0:P], 8), s, negmax[:, u % 2, 0:8].unsqueeze(2).broadcast_to([P, 8, NC]),
                   ALU.add).then_inc(s_max, 1)

            def unit_scale(g, i):
                u = UNITS[g] + i
                dve.wait_ge(s_exp, u + 1)
                gate = {"cmp": 0, "sel": 1, "win": 2}.get(g)
                if g == "cmp":
                    qt, hs = i, range(8)
                    link(dve.tensor_reduce(rsum[:, qt, :], heads(p_of(u)[:, 0:P], 8), AX.X, ALU.add))
                else:
                    qt, hs = GROUP[i]
                w = wgt[:, qt, hs[0]:hs[-1] + 1]
                link(dve.reciprocal(w, rsum[:, qt, hs[0]:hs[-1] + 1]))
                if g == "cmp":
                    link(ts(w, w, con("valid")[:, qt:qt + 1], None, ALU.mult))
                if gate is not None:
                    link(tt(w, w, gates[:, qt, gate * 8 + hs[0]:gate * 8 + hs[-1] + 1], ALU.mult))
                p = heads(p_of(u)[:, 0:P if g == "cmp" else 512], len(hs))
                tt(p, p, w.unsqueeze(2).broadcast_to([P, len(hs), p.shape[2]]), ALU.mult).then_inc(s_scaled, 1)

            def attention(l, between):
                units = CHAINS[l]
                for n in range(len(units) + 3):
                    if n < len(units):
                        g, i = units[n]
                        compressed_max(i) if g == "cmp" else unit_max(g, i)
                    if 0 <= n - 1 < len(units):
                        unit_scale(*units[n - 1])
                    if n >= 3:
                        g, i = units[n - 3]
                        if g in SUMS and (n - 2 == len(units) or units[n - 2][0] != g):
                            dve.wait_ge(s_pv, UNITS[g] + i + 1)
                            dve.tensor_copy(mixT[:, SUMS[g]:SUMS[g] + 4, P:T],
                                            o_bank[1][:, :].rearrange("p (k q) -> p k q", k=4)).then_inc(o_taken[1], 1)
                    for f in between.get(n, ()):
                        f()

            def residual(t, n, src):
                xs = x[:, t, n * 512:(n + 1) * 512]
                return stt(xs, xs, ALPHA, src, ALU.mult, ALU.add)

            def norm_tile(t, source):
                nonlocal n_std
                halves = []
                for n in range(2):
                    halves.append(source(n))
                    ins = dve.bn_stats(stat[:, t, 6 * n:6 * n + 6], halves[n])
                link(ins)
                link(dve.bn_aggr(mv[:, t, :], stat[:, t, :]))
                dve.wait_ge(act_std, n_std)
                ts(var[:, 0:1], mv[:, t, 1:2], LN_EPS, None, ALU.add).then_inc(var_ready, 1)
                n_std += 1
                if t == 0:
                    dve.wait_ge(ln_in, 32 * (n_ln + 1))
                for n in range(2):
                    c = slice(n * 512, (n + 1) * 512)
                    ins = stt(x[:, t, c], halves[n], mv[:, t, 0:1], lnp[:, 0, c], ALU.subtract, ALU.mult)
                link(ins)
                dve.wait_ge(act_std, n_std)
                link(dve.reciprocal(rstd[:, 0:1], std[:, 0:1]))
                stt(x[:, t, :], x[:, t, :], rstd[:, 0:1], lnp[:, 1, :], ALU.mult, ALU.add).then_inc(x_ready, 1)

            def norm_end():
                nonlocal n_ln
                n_ln += 1
                dve.wait_ge(x_ready, n_ln * NT)
                dve.engine_nop().then_inc(ln_used, 1)

            for l in range(2):
                S = L[l]
                for kh in range(2):
                    take((l, "xT", 1, kh), xT[:, 4 * kh:4 * kh + 4, P:T], lambda w: w[:, :].rearrange("p (k n) -> p k n", k=4))
                if l == 0:
                    dve.tensor_copy(identb[:, :], ident)
                    dve.wait_ge(masks_in, 32)
                    dve.tensor_copy(maskb[:, :], scratch[:, 0:N_MASK]).then_inc(masks_cast, 1)
                    dve.wait_ge(masks_cast, 1)
                    take((0, "proj", 0, 1), proj[:, 1, 0:512])
                    copied((0, "proj", 0, 0))
                    copied((0, "proj", 0, 1))
                    for t in range(NT):
                        link(rope(heads(qr[:, t, :], 8), heads(proj[:, t, C_Q:C_Q + 512], 8), rope64[:, t], 8, HD))
                    dve.engine_nop().then_inc(roped, 1)

                    def rope_keys(i, a):
                        for t in range(NT):
                            link(rope(heads(kr0[:, t, i * P:(i + 1) * P], 2), heads(proj[:, t, a:a + P], 2), rope64[:, t], 2, HD))
                        dve.engine_nop().then_inc(roped, 1)
                    dve.tensor_copy(kv_pairs(1), full((0, "proj", 1, 1))[:, 0:256].rearrange("p (a g d) -> p a g d", a=2, g=G))
                    take((0, "proj", 1, 1), proj[:, 1, C_KS:C_KW], lambda b: b[:, 256:512])
                    copied((0, "proj", 1, 0))
                    copied((0, "proj", 1, 1))
                    rope_keys(0, C_KS)
                    for h in range(2):
                        take((0, "qT", 1, h), qT[0:64, 4 * h:4 * h + 4, P:T],
                             lambda w: w[0:64, :].rearrange("p (h n) -> p h n", h=4), scale=HD ** -0.5)
                    take((0, "kcvc"), kcvcT, lambda w: w[:, :].rearrange("p (g n) -> p g n", g=G))
                    copied((0, "kcvc"))
                    dve.memset(blocks[0:64, :, 1], 0.0)
                    dve.memset(blocks[64:128, :, 0], 0.0)
                    for a in range(2):
                        ins = dve.memset(blocks[64 * a:64 * a + 64, :, a, :, N_CMP:NC], 0.0)
                    link(ins)
                    for a in range(2):
                        r = slice(64 * a, 64 * a + 64)
                        for g in range(G):
                            for hl in range(2):
                                tok = kcvcT[r, g, hl * 16:hl * 16 + N_CMP * 16].rearrange("p (c l) -> p l c", l=16)
                                link(tt(blocks[r, hl * 16:hl * 16 + 16, a, g, 0:N_CMP], tok,
                                        pe_sb[r, hl * 16:hl * 16 + 16].unsqueeze(2).broadcast_to([64, 16, N_CMP]), ALU.add))
                    dve.engine_nop().then_inc(roped, 1)
                    take((0, "proj", 2, 1), proj[:, 1, 1024:1536])
                    copied((0, "proj", 2, 0))
                    copied((0, "proj", 2, 1))
                    rope_keys(1, C_KW)
                    take((0, "proj", 3, 1), proj[:, 1, 1536:W_IN], lambda b: b[:, 0:W_IN - 1536])
                    copied((0, "proj", 3, 0))
                    copied((0, "proj", 3, 1))
                    for t in range(NT):
                        for i, (a, w) in enumerate(((C_CQ, QR), (C_CKV, KVR))):
                            link(dve.tensor_tensor_reduce(tmp[:, 0, 0:w], proj[:, t, a:a + w], proj[:, t, a:a + w], 1.0 / w,
                                                          RMS_EPS, ALU.mult, ALU.add, var[:, 2 * t + i:2 * t + i + 1]))
                    dve.engine_nop().then_inc(var_ready, 1)
                    dve.wait_ge(act_std, 1)
                    n_std = 1
                    link(dve.reciprocal(rstd[:, :], std[:, :]))
                    m5 = chunk_landed(dve, 5)
                    for t in range(NT):
                        for i, (a, w, g, dst) in enumerate(((C_CQ, QR, 2688, cqn), (C_CKV, KVR, 2944, ckvn))):
                            link(stt(dst[:, t, :], proj[:, t, a:a + w], rstd[:, 2 * t + i:2 * t + i + 1],
                                     m5[:, g:g + w], ALU.mult, ALU.mult))
                    dve.engine_nop().then_inc(roped, 1)
                    dve.wait_ge(act_gate, 1)
                    link(ts(gates[:, :, :], gates[:, :, :], 1.0, None, ALU.add))
                    link(dve.reciprocal(gates[:, :, :], gates[:, :, :]))

                    take((0, "hid"), hx, lambda w: w[0:64, 0:P])
                    copied((0, "hid"))
                    link(tt(hy, hx, hx, ALU.mult))
                    link(ts(hy, hy, 0.044715, 1.0, ALU.mult, ALU.add))
                    link(tt(hy, hy, hx, ALU.mult))
                    dve.engine_nop().then_inc(act_hid, 1)

                    def gelu():
                        dve.wait_ge(act_gate, 2)
                        link(ts(hz, hz, 1.0, None, ALU.add))
                        link(dve.reciprocal(hz, hz))
                        link(tt(hx, hx, hz, ALU.mult))
                        dve.engine_nop().then_inc(roped, 1)

                    def hidden():
                        take((0, "hkT"), hk, lambda w: w[:, 0:64])
                        copied((0, "hkT"))
                        link(dve.tensor_copy(tmp[:, 0, 0:128].rearrange("p (g r c) -> p g r c", g=G, r=R),
                                             hk[:, 32:64].rearrange("p (g c) -> p g c", g=G).unsqueeze(2).broadcast_to([P, G, R, NC])))
                        dve.engine_nop().then_inc(hid_in, 1)

                    def compressed():
                        w = full((0, "kcmp"))
                        dve.tensor_copy(kc, w[0:32, 0:64])
                        free(dve.tensor_copy(vrep, w[:, 64:128]), (0, "kcmp"))
                        copied((0, "kcmp"))
                        link(rope(kcr.unsqueeze(1), kc.unsqueeze(1), ropec, 1, HD))
                        dve.engine_nop().then_inc(roped, 1)
                        link(tt(vbd, vrep.unsqueeze(1).broadcast_to([P, 8, HD]),
                                con("diag").unsqueeze(2).broadcast_to([P, 8, HD]), ALU.mult))
                        dve.engine_nop().then_inc(roped, 1)

                    def compressed_keys():
                        take((0, "kcmpT"), kcmpT, lambda w: w[0:64, 0:32])

                    def mla_queries():
                        for half in range(2):
                            take((0, "uq", 1, half), mlaq[:, 1, 4 * half:4 * half + 4, :],
                                 lambda w: w[:, 0:384].rearrange("p (h n) -> p h n", h=4), scale=QK ** -0.5)
                        for half in range(2):
                            copied((0, "uq", 0, half))
                            copied((0, "uq", 1, half))

                    def rope_mla_queries():
                        for t in range(NT):
                            q = mlaq[:, t, :, NOPE:QK]
                            link(rope(q, q, rope32[:, t], 8, ROPE_D))
                        dve.engine_nop().then_inc(roped, 1)

                    def mla_keys():
                        for half in range(2):
                            take((0, "ukv", 1, half), ukv[:, 1, half * 512:(half + 1) * 512])
                        for half in range(2):
                            copied((0, "ukv", 0, half))
                            copied((0, "ukv", 1, half))
                        for t in range(NT):
                            kv = heads(ukv[:, t, :], 8)
                            dve.tensor_copy(kfull[:, t, :, 0:NOPE], kv[:, :, 0:NOPE])
                            link(rope(heads(krope[:, t, :], 1), heads(proj[:, t, C_KR:C_KR + ROPE_D], 1), rope32[:, t], 1, ROPE_D))
                            link(dve.tensor_copy(kfull[:, t, :, NOPE:QK],
                                                 krope[:, t, :].unsqueeze(1).broadcast_to([P, 8, ROPE_D])))
                        dve.engine_nop().then_inc(roped, 1)

                    def turned(name, dst):
                        def run():
                            for h in range(2):
                                take((0, name, 1, h), dst[0:QK, 4 * h:4 * h + 4, P:T],
                                     lambda w: w[0:QK, :].rearrange("p (h n) -> p h n", h=4))
                        return run
                    attention(0, {0: (gelu,), 2: (hidden,), 3: (compressed,), 4: (compressed_keys,), 6: (mla_queries,),
                                  7: (rope_mla_queries,), 8: (mla_keys,), 10: (turned("mkT", kT),),
                                  12: (turned("mqT", mq),)})
                else:
                    for half in range(2):
                        def rope_halves(c, dst):
                            for t in range(NT):
                                stage = (1, "proj", 3 * half + c, t)
                                free(rope(heads(dst[:, t, :], 8), heads(full(stage)[:, :], 8), rope64[:, t], 8, HD), stage)
                                copied(stage)
                            dve.engine_nop().then_inc(roped, 1)
                        rope_halves(0, qr1)
                        rope_halves(1, kr1)
                        take((1, "proj", 3 * half + 2, 1), vmoba[:, half, 1, :])
                        for h in range(2):
                            take((1, "qT", half, 1, h), qTh[half][0:HD, 4 * h:4 * h + 4, P:T],
                                 lambda w: w[0:HD, :].rearrange("p (h n) -> p h n", h=4), scale=HD ** -0.5)
                        for h in range(2):
                            take((1, "kT", half, 1, h), kTh[half][0:HD, 4 * h:4 * h + 4, P:T],
                                 lambda w: w[0:HD, :].rearrange("p (h n) -> p h n", h=4))
                    attention(1, {})

                def add_output(t):
                    def run(n):
                        free(residual(t, n, full((l, "out", n, t))[:, :]), (l, "out", n, t))
                        copied((l, "out", n, t))
                        return x[:, t, n * 512:(n + 1) * 512]
                    return run
                for t in range(NT):
                    norm_tile(t, add_output(t))
                norm_end()
                for kh in range(2):
                    take((l, "yT", 1, kh), xT[:, 4 * kh:4 * kh + 4, P:T],
                         lambda w: w[:, :].rearrange("p (k n) -> p k n", k=4))
                for part in range(2):
                    for t in range(NT):
                        n_split += 1
                        dve.wait_ge(part_ready, n_split + NT * l)
                        tt(rest[:, t, :], (x, rest)[part][:, t, :], xb[:, part, t, :], ALU.subtract).then_inc(rest_ready, 1)
                dve.wait_ge(sig_ready, l + 1)
                link(ts(score, score, 1.0, None, ALU.add))
                ins = dve.reciprocal(score, score)
                free(ins, (l, "router"))
                copied((l, "router"))
                bias = chunk_landed(dve, 8 + 9 * l)[:, 512:576]
                link(tt(choice, score, bias.unsqueeze(1).broadcast_to([P, NT, E_N]), ALU.add))
                flat = choice.rearrange("p t (g n) -> p (t g) n", n=8)
                for i in range(16):
                    ins = dve.max(best8[:, i, :], flat[:, i, :])
                link(ins)
                gs = grp.rearrange("p (t g) -> p t g", t=NT)
                link(tt(grp, best8[:, :, 0], best8[:, :, 1], ALU.add))
                other = gs.unsqueeze(2).broadcast_to([P, NT, 8, 8])
                own = gs.unsqueeze(3).broadcast_to([P, NT, 8, 8])
                a4 = cmpA.rearrange("p (t i j) -> p t i j", t=NT, i=8)
                b4 = cmpB.rearrange("p (t i j) -> p t i j", t=NT, i=8)
                link(tt(b4, other, own, ALU.is_equal))
                link(tt(cmpB.rearrange("p (t n) -> p t n", t=NT), cmpB.rearrange("p (t n) -> p t n", t=NT),
                        con("lower").unsqueeze(1).broadcast_to([P, NT, 64]), ALU.mult))
                link(tt(a4, other, own, ALU.is_gt))
                link(tt(cmpA, cmpA, cmpB, ALU.add))
                link(dve.tensor_reduce(gmask, cmpA.rearrange("p (g j) -> p g j", j=8), AX.X, ALU.add))
                link(ts(gmask, gmask, TOPG - 0.5, None, ALU.is_lt))
                ts(pen, gmask, -NEG, NEG, ALU.mult, ALU.add)
                mf = masked.rearrange("p t (g n) -> p (t g) n", n=8)
                link(tt(mf, flat, gmask.unsqueeze(2).broadcast_to([P, 16, 8]), ALU.mult))
                link(tt(mf, mf, pen.unsqueeze(2).broadcast_to([P, 16, 8]), ALU.add))
                for t in range(NT):
                    link(dve.max(top8[:, 8 * t:8 * t + 8], masked[:, t, :]))
                    link(dve.match_replace(replaced[:, t, :], top8[:, 8 * t:8 * t + 8], masked[:, t, :], HIDE))
                link(ts(picked, replaced, HIDE, None, ALU.is_equal))
                dve.engine_nop().then_inc(picked_ready, 1)
                link(tt(gate_w, score, picked, ALU.mult))
                link(dve.tensor_reduce(wsum[:, 0:2], gate_w, AX.X, ALU.add))
                link(dve.reciprocal(wsum[:, 2:4], wsum[:, 0:2]))
                for t in range(NT):
                    link(ts(gate_w[:, t, :], gate_w[:, t, :], wsum[:, 2 + t:3 + t], 2.5, ALU.mult, ALU.mult))
                w = full((l, "rank"))
                r2 = w[:, 0:128].rearrange("p (t e) -> p t e", t=NT)
                link(stt(rank, r2, 1000.0, picked, ALU.add, ALU.mult))
                link(ts(rank, rank, -1000.0, None, ALU.add))
                link(dve.tensor_reduce(nwin_f[:, 0:1], w[:, 128:192], AX.X, ALU.max))
                link(ts(nwin_f[:, 1:2], nwin_f[:, 0:1], float(CAP), 1.0, ALU.is_gt, ALU.add))
                link(stt(nwin_f[:, 2:3], nwin_f[:, 0:1], 2.0 * CAP, nwin_f[:, 1:2], ALU.is_gt, ALU.add))
                ins = stt(nwin_i[:, :], nwin_f[:, 0:1], 3.0 * CAP, nwin_f[:, 2:3], ALU.is_gt, ALU.add)
                free(ins, (l, "rank"))
                copied((l, "rank"))
                dve.engine_nop().then_inc(routed, 1)
                windows = dve.value_load(nwin_i[0:1, 0:1], min_val=1, max_val=4)

                def make_sel(pair0):
                    shape = [P, NT, 2, CAP]
                    two = bass.ds(pair0 * 2, 2)
                    iota = con("iota").unsqueeze(1).unsqueeze(1).broadcast_to(shape)
                    b4 = selb.rearrange("p t (b c) -> p t b c", b=2)
                    tt(b4, iota, rank[:, :, two].unsqueeze(3).broadcast_to(shape), ALU.is_equal).then_inc(S["sel_chain"], 1)
                    return b4, gate_w[:, :, two].unsqueeze(3).broadcast_to(shape)

                def make_gated(made, at):
                    dve.wait_ge(S["sel_chain"], at + 1)
                    tt(selg.rearrange("p t (b c) -> p t b c", b=2), made[0], made[1], ALU.mult).then_inc(S["sel_ready"], 1)

                def multiply(at, j):
                    dve.wait_ge(S["silu_done"], at + 1)
                    stt(h_sb, bank[1][:, FF:2 * FF], gate_of[:, j:j + 1], sil, ALU.mult, ALU.mult).then_inc(S["h_ready"], 1)

                def make_selT(buf):
                    ts(selT[:, buf, :], comb[:, 1 - buf, T:2 * T], 0.0, None, ALU.is_gt).then_inc(S["selT_ready"], 1)

                def take_xg(at):
                    dve.wait_ge(S["xg_full"], at * 2 + 2)
                    dve.tensor_copy(xg[:, 4:8, :], bank[0][:, :].rearrange("p (k c) -> p k c", k=4)).then_inc(S["xg_copied"], 1)

                def split_y(at):
                    for n in range(2):
                        dve.wait_ge(S["y_part"], at * 4 + (n + 1))
                        tt(y_rest[:, n, :], s_bank[n][:, :], yb[:, 0, n * 512:(n + 1) * 512], ALU.subtract).then_inc(S["y_left"], 1)
                    for n in range(2):
                        dve.wait_ge(S["y_part"], at * 4 + (n + 3))
                        tt(yb[:, 2, n * 512:(n + 1) * 512], y_rest[:, n, :], yb[:, 1, n * 512:(n + 1) * 512],
                           ALU.subtract).then_inc(S["y_split"], 1)

                def pair(w, i, j, ahead=2):
                    at = w * PAIRS + i * 2 + j
                    multiply(at, j)
                    if ahead:
                        take_xg(at + 1)
                    if ahead == 2:
                        make_gated(make_sel(i * 2 + (j + 2)), at + 2)
                    if ahead:
                        dve.wait_ge(S["ht_copied"], at + 1)
                        make_selT(1 - j)
                    split_y(at)

                make_gated(make_sel(0), 0)
                dve.wait_ge(sh_silu, l + 1)
                tt(h_sh.rearrange("p j t -> p (j t)"), s_bank[1][:, :], sil_sh, ALU.mult).then_inc(sh_h, 1)
                with dve.Fori(0, windows) as w:
                    take_xg(w * PAIRS)
                    make_gated(make_sel(1), w * PAIRS + 1)
                    dve.wait_ge(S["sel0_copied"], w + 1)
                    make_selT(0)
                    with dve.Fori(0, 15) as i:
                        for j in range(2):
                            pair(w, i, j)
                    for j in range(2):
                        pair(w, 15, j, ahead=1 - j)
                    ts(rank, rank, -float(CAP), None, ALU.add).then_inc(S["rank_moved"], 1)
                    dve.wait_ge(S["rank_moved"], w + 1)
                    make_gated(make_sel(0), (w + 1) * PAIRS)
                    dve.wait_ge(S["window_done"], w + 1)
                dve.engine_nop().then_inc(experts_done, 1)
                for t in range(NT):
                    norm_tile(t, lambda n, t=t: bank[4 + 2 * t + n][:, :])
                norm_end()


_INS = ["x"] + ["l0_" + n for n in (
    "w_in", "nsa_cmp_k1", "nsa_cmp_k2", "nsa_cmp_v1", "nsa_cmp_v2", "mla_q_norm", "mla_w_uq", "mla_kv_norm",
    "mla_w_ukv")] + ["l1_w_qkv"] + [f"l{l}_{n}" for l in range(2) for n in (
        "w_out", "ln1_g", "ln1_b", "router", "router_bias", "exp_gate", "exp_up", "exp_down", "sh_gate", "sh_up",
        "sh_down", "ln2_g", "ln2_b")]


def rope_table(pos, d):
    half = d // 2
    inv = (np.float32(10000.0) ** (-np.arange(half, dtype=np.float32) / np.float32(half))).astype(np.float32)
    ang = (pos.astype(np.float32)[:, None] * inv[None, :]).astype(np.float64)
    c, s = np.cos(ang), np.sin(ang)
    return np.stack([np.concatenate([c, c], -1), np.concatenate([-s, s], -1)], 1).astype(np.float32)


def constants():
    p = np.arange(P)
    f = {"ident": np.eye(P), "alpha": ALPHA * np.eye(P), "before": (p[:, None] < p[None, :]), "ones": np.ones((P, P)),
         "iota": np.tile(np.arange(CAP), (P, 1)),
         "lower": np.tile((np.arange(8)[None, :] < np.arange(8)[:, None]).reshape(1, 64), (P, 1)),
         "diag": (p[:, None] // NC == np.arange(8)[None, :]),
         "valid": (p[:, None] + P * np.arange(NT)[None, :] >= CMP_LEN - 1)}
    for d in (64, 32):
        f[f"rope{d}"] = np.concatenate([rope_table(t * P + p, d).reshape(P, 2 * d) for t in range(NT)], 1)
    ends = np.tile(np.arange(NC) * CMP_STRIDE + CMP_LEN - 1, G)
    f["ropec"] = np.concatenate([rope_table(ends, 64).reshape(32, 128), np.zeros((P - 32, 128))], 0)
    tab = np.zeros((P, N_CONST), np.float32)
    for n, (a, w) in CONST.items():
        tab[:, a:a + w] = f[n]
    mask = np.zeros((P, N_MASK), np.float32)
    mask[:, 128:256] = np.where(p[None, :] > p[:, None], NEG, 0.0)
    c = p % NC
    for qt in range(NT):
        seen = (c[None, :] * CMP_STRIDE + CMP_LEN - 1 <= qt * P + p[:, None]) & (c[None, :] < N_CMP)
        mask[:, 256 + qt * P:256 + (qt + 1) * P] = np.where(seen, 0.0, NEG)
    return tab, mask


def kernel(**inputs):
    import concourse.bacc as _bacc
    from concourse import mybir as _mybir
    from concourse.bass_utils import run_bass_kernel_spmd as _run

    nc = _bacc.Bacc("TRN2", target_bir_lowering=False, num_devices=1)
    arrays, A = {}, {}

    def declare(name, a):
        a = np.ascontiguousarray(a)
        arrays[f"in_{name}_dram"] = a
        return nc.dram_tensor(f"in_{name}_dram", a.shape, _mybir.dt.from_np(a.dtype), kind="ExternalInput").ap()

    for name in _INS:
        A[name] = declare(name, inputs[name])
    peT = declare("peT", np.concatenate([np.asarray(inputs["l0_nsa_pe_k"]).T, np.asarray(inputs["l0_nsa_pe_v"]).T], 0))
    tab, mask = constants()
    table, masks = declare("table", tab), declare("masks", mask)
    out = nc.dram_tensor("out_0_dram", (1, T, D), _mybir.dt.from_np(np.dtype("float32")), kind="ExternalOutput").ap()
    build(nc, A, table, masks, peT, out)
    r = _run(nc, [arrays], core_ids=[0])
    return r.results[0]["out_0_dram"]
```
